# Optimizing a Trainium2 kernel written in Bass

```python
import jax, jax.numpy as jnp
from jax import lax
import numpy as np

D_MODEL = 1024
BATCH = 1
SEQ = 2048
DEPTH = 1

NORM_EPS = 1e-6
D_MIX = 2 * D_MODEL
GLA_HEADS = 4
GLA_DK = D_MODEL // (2 * GLA_HEADS)
GLA_DV = D_MODEL // GLA_HEADS
GLA_KEY = GLA_HEADS * GLA_DK
GLA_VAL = GLA_HEADS * GLA_DV
GLA_GATE_RANK = 16
GLA_TAU = 16.0
GLA_CHUNK = 64
SSD_INNER = D_MIX - GLA_VAL
SSD_HEAD_DIM = 64
SSD_HEADS = SSD_INNER // SSD_HEAD_DIM
SSD_GROUPS = 2
SSD_STATE = 128
SSD_CONV = 4
SSD_CHUNK = 128
SSD_CONV_DIM = SSD_INNER + 2 * SSD_GROUPS * SSD_STATE
PROJ_SIZES = (GLA_KEY, GLA_KEY, GLA_VAL, GLA_VAL, GLA_GATE_RANK,
              SSD_INNER, SSD_CONV_DIM, SSD_HEADS)
D_PROJ = sum(PROJ_SIZES)
PROJ_SPLITS = tuple(sum(PROJ_SIZES[:i + 1]) for i in range(len(PROJ_SIZES) - 1))

kernel_name = "hybrid_gla_ssd_parallel_heads"

def rms_norm(x, w, eps=NORM_EPS):
    xf = x.astype(jnp.float32)
    y = xf * lax.rsqrt(jnp.mean(xf * xf, axis=-1, keepdims=True) + eps)
    return (y * w.astype(jnp.float32)).astype(x.dtype)

def causal_depthwise_conv(u, w, b):
    out = lax.conv_general_dilated(
        u, w[:, None, :], window_strides=(1,), padding=[(w.shape[0] - 1, 0)],
        dimension_numbers=('NWC', 'WIO', 'NWC'), feature_group_count=u.shape[-1])
    return out + b

def gla_chunked(q, k, v, log_a):
    Bsz, T, H, K = q.shape
    V = v.shape[-1]
    C = GLA_CHUNK
    N = T // C
    q, k, log_a = [t.reshape(Bsz, N, C, H, K) for t in (q, k, log_a)]
    v = v.reshape(Bsz, N, C, H, V)
    b = jnp.cumsum(log_a, axis=2)
    b_last = b[:, :, -1:]
    q_dec = q * jnp.exp(b)
    k_dec = k * jnp.exp(-b)
    k_end = k * jnp.exp(b_last - b)
    causal = jnp.tril(jnp.ones((C, C), dtype=bool))
    att = jnp.einsum('bnihk,bnjhk->bnhij', q_dec, k_dec)
    att = jnp.where(causal, att, 0.0)
    o = jnp.einsum('bnhij,bnjhv->bnihv', att, v)
    kv = jnp.einsum('bnjhk,bnjhv->bnhkv', k_end, v)
    decay = jnp.exp(b_last[:, :, 0])

    def step(S, inp):
        kv_n, d_n = inp
        return S * d_n[..., None] + kv_n, S

    S0 = jnp.zeros((Bsz, H, K, V), q.dtype)
    _, S_prev = lax.scan(step, S0, (jnp.moveaxis(kv, 1, 0), jnp.moveaxis(decay, 1, 0)))
    S_prev = jnp.moveaxis(S_prev, 0, 1)
    o = o + jnp.einsum('bnihk,bnhkv->bnihv', q_dec, S_prev)
    return o.reshape(Bsz, T, H, V)

def ssd_chunked(x, dt, A, Bm, Cm):
    Bsz, T, H, P = x.shape
    G, N = Bm.shape[2], Bm.shape[3]
    Hg = H // G
    L = SSD_CHUNK
    nc = T // L
    x = x.reshape(Bsz, nc, L, G, Hg, P)
    dt = dt.reshape(Bsz, nc, L, G, Hg)
    Bm = Bm.reshape(Bsz, nc, L, G, N)
    Cm = Cm.reshape(Bsz, nc, L, G, N)
    a_cum = jnp.cumsum(dt * A.reshape(G, Hg), axis=2)
    causal = jnp.tril(jnp.ones((L, L), dtype=bool))
    seg = a_cum[:, :, :, None] - a_cum[:, :, None]
    decay_ij = jnp.exp(jnp.where(causal[:, :, None, None], seg, -jnp.inf))
    cb = jnp.einsum('bcign,bcjgn->bcijg', Cm, Bm)
    w = cb[..., None] * decay_ij * dt[:, :, None]
    y = jnp.einsum('bcijgh,bcjghp->bcighp', w, x)
    decay_end = jnp.exp(a_cum[:, :, -1:] - a_cum)
    states = jnp.einsum('bcjgn,bcjghp->bcghpn', Bm, (decay_end * dt)[..., None] * x)
    chunk_decay = jnp.exp(a_cum[:, :, -1])

    def step(S, inp):
        st, d = inp
        return S * d[..., None, None] + st, S

    S0 = jnp.zeros((Bsz, G, Hg, P, N), x.dtype)
    _, S_prev = lax.scan(step, S0, (jnp.moveaxis(states, 1, 0), jnp.moveaxis(chunk_decay, 1, 0)))
    S_prev = jnp.moveaxis(S_prev, 0, 1)
    y = y + jnp.einsum('bcign,bcghpn,bcigh->bcighp', Cm, S_prev, jnp.exp(a_cum))
    return y.reshape(Bsz, T, H, P)

def setup_inputs(seed: int = 0) -> dict:
    key = jax.random.key(seed)
    ks = jax.random.split(key, 20)
    f32 = jnp.float32
    nrm = lambda k, shape, s: jax.random.normal(k, shape, f32) * s
    dt0 = jnp.exp(jax.random.uniform(ks[10], (DEPTH, SSD_HEADS), f32,
                                     np.log(1e-3).astype(np.float32), np.log(1e-1).astype(np.float32)))
    return {
        "x": nrm(ks[0], (BATCH, SEQ, D_MODEL), 1.0),
        "c": nrm(ks[1], (BATCH, D_MODEL), 1.0),
        "ada_w": nrm(ks[2], (DEPTH, D_MODEL, 3 * D_MODEL), D_MODEL ** -0.5),
        "ada_b": nrm(ks[3], (DEPTH, 3 * D_MODEL), 0.01),
        "pre_norm_w": 1.0 + nrm(ks[4], (DEPTH, D_MODEL), 0.1),
        "w_in": nrm(ks[5], (DEPTH, D_MODEL, D_PROJ), D_MODEL ** -0.5),
        "gla_gate_w2": nrm(ks[6], (DEPTH, GLA_GATE_RANK, GLA_KEY), GLA_GATE_RANK ** -0.5),
        "gla_gate_b": nrm(ks[7], (DEPTH, GLA_KEY), 0.1),
        "gla_norm_w": 1.0 + nrm(ks[8], (DEPTH, GLA_DV), 0.1),
        "conv_w": nrm(ks[9], (DEPTH, SSD_CONV, SSD_CONV_DIM), SSD_CONV ** -0.5),
        "conv_b": nrm(ks[11], (DEPTH, SSD_CONV_DIM), 0.01),
        "dt_bias": dt0 + jnp.log(-jnp.expm1(-dt0)),
        "a_log": jnp.log(jax.random.uniform(ks[12], (DEPTH, SSD_HEADS), f32, 1.0, 16.0)),
        "d_skip": 1.0 + nrm(ks[13], (DEPTH, SSD_HEADS), 0.1),
        "ssd_norm_w": 1.0 + nrm(ks[14], (DEPTH, SSD_INNER), 0.1),
        "w_out": nrm(ks[15], (DEPTH, D_MIX, D_MODEL), D_MIX ** -0.5),
        "post_norm_w": 1.0 + nrm(ks[16], (DEPTH, D_MODEL), 0.1),
    }

def reference(x, c, ada_w, ada_b, pre_norm_w, w_in, gla_gate_w2, gla_gate_b, gla_norm_w,
              conv_w, conv_b, dt_bias, a_log, d_skip, ssd_norm_w, w_out, post_norm_w):
    f32 = jnp.float32
    Bsz, T, _ = x.shape
    c_act = jax.nn.silu(c)
    for i in range(DEPTH):
        ada = c_act @ ada_w[i] + ada_b[i]
        shift, scale, gate = jnp.split(ada, 3, axis=-1)
        h = rms_norm(x, pre_norm_w[i]) * (1.0 + scale[:, None]) + shift[:, None]
        proj = h @ w_in[i]
        q, k, v, g, gate_lr, z, xbc, dt_raw = jnp.split(proj, PROJ_SPLITS, axis=-1)

        qh = q.reshape(Bsz, T, GLA_HEADS, GLA_DK).astype(f32) * (GLA_DK ** -0.5)
        kh = k.reshape(Bsz, T, GLA_HEADS, GLA_DK).astype(f32)
        vh = v.reshape(Bsz, T, GLA_HEADS, GLA_DV).astype(f32)
        log_a = jax.nn.log_sigmoid((gate_lr @ gla_gate_w2[i] + gla_gate_b[i]).astype(f32)) / GLA_TAU
        o = gla_chunked(qh, kh, vh, log_a.reshape(Bsz, T, GLA_HEADS, GLA_DK))
        o = rms_norm(o, gla_norm_w[i]).astype(x.dtype).reshape(Bsz, T, GLA_VAL)
        o = o * jax.nn.silu(g)

        xbc = jax.nn.silu(causal_depthwise_conv(xbc, conv_w[i], conv_b[i]))
        xs, Bm, Cm = jnp.split(xbc, [SSD_INNER, SSD_INNER + SSD_GROUPS * SSD_STATE], axis=-1)
        dt = jax.nn.softplus(dt_raw.astype(f32) + dt_bias[i].astype(f32))
        A = -jnp.exp(a_log[i].astype(f32))
        xs_h = xs.reshape(Bsz, T, SSD_HEADS, SSD_HEAD_DIM).astype(f32)
        y = ssd_chunked(xs_h, dt, A,
                        Bm.reshape(Bsz, T, SSD_GROUPS, SSD_STATE).astype(f32),
                        Cm.reshape(Bsz, T, SSD_GROUPS, SSD_STATE).astype(f32))
        y = y + d_skip[i].astype(f32)[:, None] * xs_h
        y = y.reshape(Bsz, T, SSD_INNER).astype(x.dtype) * jax.nn.silu(z)
        y = rms_norm(y.reshape(Bsz, T, SSD_GROUPS, SSD_INNER // SSD_GROUPS),
                     ssd_norm_w[i].reshape(SSD_GROUPS, SSD_INNER // SSD_GROUPS))
        y = y.reshape(Bsz, T, SSD_INNER)

        mixed = jnp.concatenate([o, y], axis=-1) @ w_out[i]
        x = x + gate[:, None] * rms_norm(mixed, post_norm_w[i])
    return x


_drawn_inputs = setup_inputs


def setup_inputs(seed=0):
    import zlib

    import numpy as np

    out = dict(_drawn_inputs(seed))
    spreads = {}
    factors = {'ada_b': 4.112, 'conv_b': 8.0, 'd_skip': 20.717}
    for name, (base, spread) in spreads.items():
        noise = np.random.default_rng([zlib.crc32(name.encode()), seed]).standard_normal(out[name].shape)
        drawn = base * np.exp(spread * noise) if base else spread * noise
        out[name] = __import__('jax').numpy.asarray(drawn.astype(out[name].dtype))
    for name, factor in factors.items():
        out[name] = (out[name] * factor).astype(out[name].dtype)
    return out
```

```python
from contextlib import ExitStack

import concourse.bass as bass
from concourse import mybir

F32 = mybir.dt.float32
F32R = mybir.dt.float32r
I32 = mybir.dt.int32
ALU = mybir.AluOpType
ACT = mybir.ActivationFunctionType

P = 128
HI, LO = 0, 1
PASSES = ((HI, HI), (HI, LO), (LO, HI))
EPS = 1e-6


def wait(eng, sem, count):
    if not isinstance(count, int) or count > 0:
        eng.wait_ge(sem, count)


def build(nc, x, c, ada_w, ada_b, pre_norm_w, w_in, gla_gate_w2, gla_gate_b, gla_norm_w, conv_w, conv_b,
          dt_bias, a_log, d_skip, ssd_norm_w, w_out, post_norm_w, out):
    _, T, D = x.shape
    KT = D // P
    RANK, KEY = gla_gate_w2.shape[1:]
    DK = P
    GH = KEY // DK
    DV = gla_norm_w.shape[1]
    VAL = GH * DV
    SH = dt_bias.shape[1]
    SP_ = ssd_norm_w.shape[1] // SH
    INNER = SH * SP_
    TAPS, CONV = conv_w.shape[1:]
    NS = P
    G = (CONV - INNER) // (2 * NS)
    HG = SH // G
    GW = INNER // G
    XT = GW // P
    FT = (VAL + INNER) // P
    CH = 64
    assert DK ** -0.5 * (2 * DK) ** 0.5 > 1 and DV == 2 * P and D == 1024 and SH == RANK == 16
    CQ, CK, CV = 0, KEY, 2 * KEY
    CG = CV + VAL
    CR = CG + VAL
    CZ = CR + RANK
    CX = CZ + INNER
    CD = CX + CONV

    B1 = 512
    NB = T // B1
    TB = B1 // P
    B2 = 256
    NB2 = T // B2
    TB2 = B2 // P

    w_rows = w_in[0].rearrange("(k p) n -> p k n", p=P)

    h_d = nc.dram_tensor("h", (NB, P, KT, B1), F32, kind="Internal").ap()
    ac_d = nc.dram_tensor("step_sums", (SH, T), F32, kind="Internal").ap()
    y_d = nc.dram_tensor("mixed_in", (NB2, P, FT, B2), F32, kind="Internal").ap()

    with ExitStack() as whole:
        def keep(name, shape, dt=F32):
            return whole.enter_context(nc.sbuf_tensor(name, shape, dt))

        ps = whole.enter_context(nc.psum_tensor("ps", [P, 8, 512], F32))
        ident = keep("ident", [P, P])
        gate_row = keep("gate_row", [P, D])
        with ExitStack() as parts:
            tok = parts.enter_context(nc.sbuf_tensor("tok", [P, T // P, 4, SH], F32))
            conv_col = parts.enter_context(nc.sbuf_tensor("conv_col", [P, TAPS, CONV // P], F32))
            convb_col = parts.enter_context(nc.sbuf_tensor("convb_col", [P, CONV // P], F32))
            d_col = parts.enter_context(nc.sbuf_tensor("d_col", [P, G * XT], F32))
            ssd_norm_col = parts.enter_context(nc.sbuf_tensor("ssd_norm_col", [P, G * XT], F32))
            with (nc.sbuf_tensor("causal", [P, P], F32) as causal,
                  nc.sbuf_tensor("keep_row", [P, B1], F32) as keep_row,
                  nc.sbuf_tensor("code", [RANK, T], F32) as code):
                prologue(nc, x, c, ada_w, ada_b, pre_norm_w, w_rows, dt_bias, a_log, post_norm_w, ps, ident, causal,
                         gate_row, keep_row, tok, code, h_d, ac_d, T, D, KT, SH, RANK, CR, CD, B1, NB, TB)
                gla(nc, w_rows, gla_gate_w2, gla_gate_b, gla_norm_w, ps, ident, causal, keep_row, code, h_d, y_d,
                    conv_w, conv_b, d_skip, ssd_norm_w, conv_col, convb_col, d_col, ssd_norm_col, KT, GH, DK, DV,
                    RANK, SP_, TAPS, CQ, CK, CV, CG, CH, B1, NB, TB, B2)
            ssd(nc, w_rows, conv_col, convb_col, d_col, ssd_norm_col, ps, ident, tok, h_d, ac_d, y_d, T, KT, G, HG, GW,
                XT, NS, SP_, INNER, VAL, TAPS, CZ, CX, B2, TB2)
        project_out(nc, x, w_out, out, ps, gate_row, y_d, D, FT, NB2, B2, TB2)


def prologue(nc, x, c, ada_w, ada_b, pre_norm_w, w_rows, dt_bias, a_log, post_norm_w, ps, ident, causal, gate_row,
             keep_row, tok, code, h_d, ac_d, T, D, KT, SH, RANK, CR, CD, B1, NB, TB):
    R0 = 32
    RS = slice(R0, R0 + SH)
    TURN, PACK, ROWS, GATE = 0, 3, 4, 5
    CODES = (2, 7)
    with ExitStack() as ctx:
        def sb(name, shape, dt=F32):
            return ctx.enter_context(nc.sbuf_tensor(name, shape, dt))

        def sem(name):
            return ctx.enter_context(nc.semaphore(name))

        ada = sb("ada", [P, KT, 2 * D])
        c_col = sb("c_col", [P, KT])
        c_act = sb("c_act", [P, KT])
        c_wide = sb("c_wide", [P, KT, P])
        one = sb("one", [1, 1])
        mod_row = ada[0:1, KT - 1, :]
        ada_col = sb("ada_col", [P, 2 * KT])
        pre_col = sb("pre_col", [P, KT])
        mod = sb("mod", [P, 2 * KT])
        gain = sb("gain", [P, KT])
        ada_row = ada[:, 0, D:2 * D]
        post_row = ada[:, 1, D:2 * D]
        x_sb = sb("x_sb", [P, NB, TB, D])
        squares = sb("squares", [P, D])
        ms = sb("ms", [P, TB])
        mse = sb("mse", [P, TB])
        rstd = sb("rstd", [P, TB])
        neg_half = sb("neg_half", [P, TB])
        hf = sb("hf", [P, 2, KT, B1])
        wg = sb("wg", [P, KT, R0 + SH])
        dtb = sb("dtb", [P, 1])
        alog = sb("alog", [P, 1])
        aexp = sb("aexp", [P, 1])
        dtx = sb("dtx", [P, B1])
        dsoft = sb("dsoft", [P, B1])
        dta = sb("dta", [P, B1])
        dlast = sb("dlast", [P, B1])
        pack = sb("pack", [P, 4, B1])

        passed = sem("a_passed")
        consts_ready = sem("a_consts"); loads = sem("a_loads"); c_loaded = sem("a_c_loaded"); cols_loaded = sem("a_cols_loaded"); wg_loaded = sem("a_wg_loaded")
        ada_loaded = [sem(f"a_ada_loaded{i}") for i in range(KT)]
        gate_loaded = sem("a_gate_loaded")
        c_ready = sem("a_c_ready"); wide_ready = sem("a_wide_ready")
        mod_done = sem("a_mod_done"); row_ready = sem("a_row_ready"); cols_done = sem("a_cols_done")
        gate_done = sem("a_gate_done"); mod_ready = sem("a_mod_ready")
        gain_ready = sem("a_gain_ready"); gate_sum = sem("a_gate_sum"); gate_ready = sem("a_gate_ready")
        aexp_ready = sem("a_aexp_ready"); a_ready = sem("a_a_ready")
        x_loaded = [sem(f"a_x_loaded{i}") for i in range(NB)]
        ms_ready = sem("a_ms_ready"); mse_ready = sem("a_mse_ready"); rstd_ready = sem("a_rstd_ready")
        xn_ready = sem("a_xn_ready"); turned = sem("a_turned")
        even_ready = sem("a_even_ready"); odd_ready = sem("a_odd_ready")
        h_stored = [sem(f"a_h_stored{i}") for i in range(2)]
        codes_done = sem("a_codes_done"); code_ready = sem("a_code_ready"); dtx_ready = sem("a_dtx_ready")
        dsoft_step = sem("a_dsoft_step"); dt_ready = sem("a_dt_ready"); dta_ready = sem("a_dta_ready")
        acum_ready = sem("a_acum_ready"); dlast_ready = sem("a_dlast_ready"); pack_ready = sem("a_pack_ready")
        acum_stored = sem("a_acum_stored"); packed = sem("a_packed"); tok_ready = sem("a_tok_ready")

        def wait_h(eng, b, k):
            wait(eng, odd_ready if k % 2 else even_ready, b * (KT // 2) + k // 2 + 1)

        def blocks(step):
            for m in range(NB):
                step(m, m % 2, m // 2, m < NB - 1)

        with nc.Block() as block:
            @block.sync
            def _(sp):
                def load_x(b):
                    sp.dma_start(x_sb[:, b], x[0, b * B1:(b + 1) * B1, :].rearrange("(t p) n -> p t n", p=P)
                                 ).then_inc(x_loaded[b], 16)

                sp.dma_start(c_col[:, :], c.rearrange("a (k p) -> p (a k)", p=P), allow_slow_non_contiguous=True).then_inc(c_loaded, 16)
                for k in range(KT):
                    sp.dma_start(ada[:, k, :], ada_w[0, k * P:(k + 1) * P, 0:2 * D]).then_inc(ada_loaded[k], 16)
                    if k == 1:
                        load_x(0)
                load_x(1)
                sp.wait_ge(mod_done, 1)
                for b in range(2, NB):
                    load_x(b)

                def step(m, par, rnd, more):
                    for half in range(2):
                        ks = slice(half * KT // 2, (half + 1) * KT // 2)
                        for k in (ks.stop - 2, ks.stop - 1):
                            wait_h(sp, m, k)
                        sp.dma_start(h_d[bass.ds(m, 1), :, ks].rearrange("a p k n -> (a p) k n"), hf[:, par, ks]
                                     ).then_inc(h_stored[par], 16)
                        if half == 0 and m == NB - 2:
                            sp.wait_ge(cols_done, 1)
                            sp.dma_start(ada[:, :, 0:D], ada_w[0, :, 2 * D:3 * D].rearrange("(k p) n -> p k n", p=P)
                                         ).then_inc(gate_loaded, 16)
                            sp.dma_start(ada_row, ada_b[0, 2 * D:3 * D].partition_broadcast(P)).then_inc(gate_loaded, 16)
                            sp.dma_start(post_row, post_norm_w[0].partition_broadcast(P)).then_inc(gate_loaded, 16)
                    if m > 0:
                        store_sums(m - 1)

                def store_sums(b):
                    sp.wait_ge(acum_ready, b + 1)
                    sp.dma_start(ac_d[:, bass.ds(b * B1, B1)], pack[RS, 1, :]).then_inc(acum_stored, 16)

                blocks(step)
                store_sums(NB - 1)
                for s in h_stored:
                    sp.wait_ge(s, 16 * NB)
                sp.wait_ge(acum_stored, 16 * NB)

            @block.gpsimd
            def _(pool):
                pool.dma_start(ada_col[:, :], ada_b[0, 0:2 * D].rearrange("(k p) -> p k", p=P), allow_slow_non_contiguous=True).then_inc(cols_loaded, 16)
                pool.dma_start(pre_col[:, :], pre_norm_w[0].rearrange("(k p) -> p k", p=P), allow_slow_non_contiguous=True).then_inc(cols_loaded, 16)
                pool.memset(ident[:, :], 0.0).then_inc(consts_ready, 1)
                pool.memset(causal[:, :], 1.0).then_inc(consts_ready, 1)
                pool.memset(keep_row[:, :], 1.0).then_inc(consts_ready, 1)
                pool.memset(neg_half[:, :], -0.5).then_inc(consts_ready, 1)
                pool.memset(wg[:, :, :], 0.0).then_inc(consts_ready, 1)
                pool.memset(one[:, :], 1.0).then_inc(consts_ready, 1)
                pool.wait_ge(consts_ready, 6)
                pool.affine_select(out=ident[:, :], in_=ident[:, :], compare_op=ALU.not_equal, fill=1.0,
                                   base=0, pattern=[[-1, P]], channel_multiplier=1).then_inc(consts_ready, 1)
                pool.affine_select(out=causal[:, :], in_=causal[:, :], compare_op=ALU.is_ge, fill=0.0,
                                   base=0, pattern=[[1, P]], channel_multiplier=-1).then_inc(consts_ready, 1)
                pool.memset(keep_row[:, :].rearrange("p (t n) -> p t n", n=P)[:, :, 0:1], 0.0).then_inc(consts_ready, 1)
                pool.dma_start(wg[:, :, 0:RANK], w_rows[:, :, CR:CR + RANK]).then_inc(wg_loaded, 16)
                pool.dma_start(wg[:, :, R0:R0 + SH], w_rows[:, :, CD:CD + SH]).then_inc(wg_loaded, 16)
                pool.dma_start(dtb[RS, :], dt_bias.rearrange("a h -> h a"), allow_slow_non_contiguous=True).then_inc(loads, 16)
                pool.dma_start(alog[RS, :], a_log.rearrange("a h -> h a"), allow_slow_non_contiguous=True).then_inc(loads, 16)

                def rstds(b):
                    pool.wait_ge(ms_ready, b * TB + TB)
                    wait(pool, xn_ready, b * TB)
                    pool.sem_inc(passed, 1)
                    pool.tensor_scalar(mse[:, :], ms[:, :], EPS, None, ALU.add).then_inc(mse_ready, 1)
                    pool.wait_ge(mse_ready, b + 1)
                    pool.tensor_tensor(rstd[:, :], mse[:, :], neg_half[:, :], ALU.pow).then_inc(rstd_ready, 1)

                rstds(0)
                with pool.Fori(1, NB) as b:
                    rstds(b)

            @block.scalar
            def _(act):
                def square(b, t):
                    if t == 0:
                        act.wait_ge(x_loaded[b], 16)
                        wait(act, mse_ready, b)
                    wait(act, ms_ready, b * TB + t)
                    act.activation(squares[:, :], x_sb[:, b, t, :], ACT.Square, scale=1.0 / 32.0,
                                   accum_out=ms[:, t:t + 1]).then_inc(ms_ready, 1)

                def soft_sizes(b):
                    act.wait_ge(dtx_ready, b + 1)
                    wait(act, dt_ready, b)
                    act.activation(dsoft[RS, :], dtx[RS, :], ACT.Abs).then_inc(dsoft_step, 1)
                    act.wait_ge(dsoft_step, b * 3 + 1)
                    act.activation(dsoft[RS, :], dsoft[RS, :], ACT.Exp, scale=-1.0).then_inc(dsoft_step, 1)
                    act.wait_ge(dsoft_step, b * 3 + 2)
                    act.activation(dsoft[RS, :], dsoft[RS, :], ACT.Ln, bias=1.0).then_inc(dsoft_step, 1)

                def size_exps(b):
                    act.wait_ge(acum_ready, b + 1)
                    wait(act, packed, b)
                    act.activation(pack[RS, 2, :], pack[RS, 1, :], ACT.Exp).then_inc(pack_ready, 1)
                    act.wait_ge(dlast_ready, b + 1)
                    act.activation(pack[RS, 3, :], dlast[RS, :], ACT.Exp).then_inc(pack_ready, 1)

                def step(m, par, rnd, more):
                    wait(act, h_stored[par], rnd * 32)
                    for k in range(KT):
                        if k % 2 == 0:
                            act.wait_ge(turned, m * KT + k + 1)
                            wait_h(act, m, k - 2) if k >= 2 else wait(act, even_ready, m * (KT // 2))
                            act.activation(hf[:, par, k, :], ps[:, TURN + k % 2, :], ACT.Identity,
                                           scale=gain[:, k:k + 1], bias=mod[:, k:k + 1]).then_inc(even_ready, 1)
                        if k < TB and more:
                            square(m + 1, k)
                        if k == 4 and m > 0:
                            soft_sizes(m - 1)
                    if m == 0:
                        act.wait_ge(loads, 32)
                        act.activation(aexp[RS, :], alog[RS, :], ACT.Exp).then_inc(aexp_ready, 1)
                    act.wait_ge(codes_done, m + 1)
                    act.activation(code[:, bass.ds(m * B1, B1)], ps[0:RANK, CODES[par], :], ACT.Copy).then_inc(code_ready, 1)
                    wait(act, dt_ready, m)
                    act.activation(dtx[RS, :], ps[RS, CODES[par], :], ACT.Identity, bias=dtb[RS, :]).then_inc(dtx_ready, 1)
                    if m > 0:
                        size_exps(m - 1)

                act.wait_ge(c_loaded, 16)
                act.activation(c_act[:, :], c_col[:, :], ACT.Silu).then_inc(c_ready, 1)
                act.preload_act_table_set("natural_log_exp_and_others")
                for t in range(TB):
                    square(0, t)
                act.wait_ge(mod_done, 1)
                act.activation(mod_row[:, 0:D], ps[0:1, ROWS:ROWS + 2, :].rearrange("p a n -> p (a n)"),
                               ACT.Copy).then_inc(row_ready, 1)
                act.wait_ge(gain_ready, 1)
                blocks(step)
                soft_sizes(NB - 1)
                size_exps(NB - 1)

            @block.vector
            def _(dve):
                def normed(b):
                    dve.wait_ge(rstd_ready, b + 1)
                    for t in range(TB):
                        dve.tensor_scalar(x_sb[:, b, t, :], x_sb[:, b, t, :], rstd[:, t:t + 1], None,
                                          ALU.mult).then_inc(xn_ready, 1)

                def sizes(b):
                    if b == 0:
                        dve.wait_ge(aexp_ready, 1)
                        dve.wait_ge(loads, 32)
                        dve.tensor_scalar(alog[RS, :], aexp[RS, :], -1.0, None, ALU.mult).then_inc(a_ready, 1)
                        dve.wait_ge(a_ready, 1)
                    dve.wait_ge(dsoft_step, b * 3 + 3)
                    wait(dve, packed, b)
                    dve.scalar_tensor_tensor(out=pack[RS, 0, :], in0=dtx[RS, :], scalar=0.0, in1=dsoft[RS, :],
                                             op0=ALU.max, op1=ALU.add).then_inc(dt_ready, 1)
                    dve.wait_ge(dt_ready, b + 1)
                    dve.tensor_scalar(dta[RS, :], pack[RS, 0, :], alog[RS, :], None, ALU.mult).then_inc(dta_ready, 1)
                    dve.wait_ge(dta_ready, b + 1)
                    wait(dve, acum_stored, b * 16)
                    dve.tensor_tensor_scan(pack[RS, 1, :], keep_row[RS, :], dta[RS, :], 0.0, ALU.mult,
                                           ALU.add).then_inc(acum_ready, 1)
                    dve.wait_ge(acum_ready, b + 1)
                    wait(dve, pack_ready, b * 2)
                    tiles = pack[RS, 1, :].rearrange("h (t n) -> h t n", n=P)
                    dve.tensor_tensor(dlast[RS, :].rearrange("h (t n) -> h t n", n=P),
                                      tiles[:, :, P - 1:P].broadcast_to([SH, TB, P]), tiles,
                                      ALU.subtract).then_inc(dlast_ready, 1)

                def keep_sizes(b):
                    dve.wait_ge(packed, b + 1)
                    dve.tensor_copy(tok[:, bass.ds(b * TB, TB), :, :].rearrange("p t q h -> p (t q h)"),
                                    ps[:, PACK, 0:TB * 4 * SH]).then_inc(tok_ready, 1)

                def step(m, par, rnd, more):
                    wait(dve, h_stored[par], rnd * 32)
                    for k in range(1, KT, 2):
                        dve.wait_ge(turned, m * KT + k + 1)
                        wait_h(dve, m, k - 2) if k >= 2 else wait(dve, odd_ready, m * (KT // 2))
                        dve.tensor_scalar(hf[:, par, k, :], ps[:, TURN + k % 2, :], gain[:, k:k + 1],
                                          mod[:, k:k + 1], ALU.mult, ALU.add).then_inc(odd_ready, 1)
                        if k == 3 and m > 1:
                            keep_sizes(m - 2)
                        if k == 5 and more:
                            normed(m + 1)
                    if m > 0:
                        sizes(m - 1)

                dve.wait_ge(c_ready, 1)
                dve.tensor_copy(c_wide[:, :, :], c_act[:, :].unsqueeze(2).broadcast_to([P, KT, P])).then_inc(wide_ready, 1)
                normed(0)
                dve.wait_ge(mod_done, 1)
                dve.tensor_copy(mod_row[:, D:2 * D], ps[0:1, ROWS + 2:ROWS + 4, :].rearrange("p a n -> p (a n)")
                                ).then_inc(row_ready, 1)
                dve.wait_ge(cols_done, 1)
                dve.wait_ge(cols_loaded, 32)
                dve.tensor_tensor(mod[:, :], ps[:, PACK, 0:2 * KT], ada_col[:, :], ALU.add).then_inc(mod_ready, 1)
                dve.wait_ge(mod_ready, 1)
                dve.scalar_tensor_tensor(out=gain[:, :], in0=mod[:, KT:2 * KT], scalar=1.0, in1=pre_col[:, :],
                                         op0=ALU.add, op1=ALU.mult).then_inc(gain_ready, 1)
                dve.wait_ge(gain_ready, 1)
                dve.wait_ge(consts_ready, 9)
                blocks(step)
                keep_sizes(NB - 2)
                sizes(NB - 1)
                dve.wait_ge(gate_done, 1)
                dve.wait_ge(gate_loaded, 48)
                dve.tensor_tensor(gate_row[:, :], ps[:, GATE:GATE + 2, :].rearrange("p a n -> p (a n)"), ada_row,
                                  ALU.add).then_inc(gate_sum, 1)
                dve.wait_ge(gate_sum, 1)
                dve.tensor_tensor(gate_row[:, :], gate_row[:, :], post_row, ALU.mult).then_inc(gate_ready, 1)
                keep_sizes(NB - 1)

            @block.tensor
            def _(pe):
                pe.wait_ge(c_ready, 1)
                for k in range(KT):
                    pe.wait_ge(ada_loaded[k], 16)
                    for j in range(2 * D // 512):
                        mm = pe.matmul(ps[0:1, ROWS + j, :], c_act[:, k:k + 1], ada[:, k, j * 512:(j + 1) * 512],
                                       start=(k == 0), stop=(k == KT - 1))
                mm.then_inc(mod_done, 1)
                pe.wait_ge(consts_ready, 9)
                pe.wait_ge(row_ready, 2)
                for f in range(2 * KT):
                    mm = pe.matmul(ps[:, PACK, f:f + 1], mod_row[:, f * P:(f + 1) * P], one[:, :], start=True, stop=True)
                mm.then_inc(cols_done, 1)
                pe.wait_ge(wg_loaded, 32)
                pe.wait_ge(mod_ready, 1)

                def codes(m, par, k):
                    wait_h(pe, m, k)
                    mm = pe.matmul(ps[0:R0 + SH, CODES[par], :], wg[:, k, :], hf[:, par, k, :],
                                   start=(k == 0), stop=(k == KT - 1))
                    if k == KT - 1:
                        mm.then_inc(codes_done, 1)

                def turn_sizes(b):
                    pe.wait_ge(pack_ready, b * 2 + 2)
                    wait(pe, tok_ready, b)
                    pe.sem_inc(passed, 1)
                    for t in range(TB):
                        for q in range(4):
                            o = (t * 4 + q) * SH
                            mm = pe.transpose(ps[:, PACK, o:o + SH], pack[RS, q, t * P:(t + 1) * P], ident[RS, RS])
                    mm.then_inc(packed, 1)

                def step(m, par, rnd, more):
                    pe.wait_ge(xn_ready, m * TB + TB)
                    wait(pe, dtx_ready, m - 1)
                    for k in range(KT):
                        if k >= 2:
                            wait_h(pe, m, k - 2)
                        elif m > 0:
                            wait_h(pe, m - 1, KT - 2 + k)
                        for t in range(TB):
                            mm = pe.transpose(ps[:, TURN + k % 2, t * P:(t + 1) * P], x_sb[:, m, t, k * P:(k + 1) * P],
                                              ident[:, :])
                        mm.then_inc(turned, 1)
                        if k > 0:
                            codes(m, par, k - 1)
                        if k == 2 and m > 1:
                            turn_sizes(m - 2)
                    codes(m, par, KT - 1)

                blocks(step)
                turn_sizes(NB - 2)
                pe.wait_ge(wide_ready, 1)
                pe.wait_ge(gate_loaded, 48)
                for j in range(2):
                    for k in range(KT):
                        mm = pe.matmul(ps[:, GATE + j, :], c_wide[:, k, :], ada[:, k, j * 512:(j + 1) * 512],
                                       start=(k == 0), stop=(k == KT - 1))
                mm.then_inc(gate_done, 1)
                turn_sizes(NB - 1)


def gla(nc, w_rows, gla_gate_w2, gla_gate_b, gla_norm_w, ps, ident, causal, keep_row, code, h_d, y_d, conv_w, conv_b,
        d_skip, ssd_norm_w, conv_col, convb_col, d_col, ssd_norm_col, KT, GH, DK, DV, RANK, SP_, TAPS, CQ, CK, CV, CG,
        CH, B1, NB, TB, B2):
    U = 6
    UQ, UK, UG, UV = 0, 1, 2, 4
    TAU = 16.0
    PROJ, KTURN, AT, O, KV, OT, GATE = 0, 2, 3, 4, 5, 6, 7
    QK = 2
    QS = KT // QK
    with ExitStack() as ctx:
        def sb(name, shape, dt=F32):
            return ctx.enter_context(nc.sbuf_tensor(name, shape, dt))

        def sem(name):
            return ctx.enter_context(nc.semaphore(name))

        hl = sb("b_hl", [P, 2, KT, 2, B1], F32R)
        w = sb("b_w", [P, UV, KT, 2, P], F32R)
        w_v = sb("b_w_v", [P, KT, 2, DV], F32R)
        w_raw = sb("b_w_raw", [P, 2, KT, P])
        h_raw = sb("b_h_raw", [P, 2, QK, B1])
        w2 = sb("b_w2", [RANK, GH * DK])
        gb = sb("b_gb", [P, GH])
        w2_h = sb("b_w2_h", [RANK, DK])
        gb_h = sb("b_gb_h", [P, 1])
        xg = sb("b_xg", [P, B1])
        soft = sb("b_soft", [P, B1])
        sums = sb("b_sums", [P, B1])
        qk = sb("b_qk", [P, 2, B1])
        gz = sb("b_gz", [P, 2, 2, B1])
        v = sb("b_v", [P, 2, TB, DV])
        e_all = sb("b_e_all", [P, B1])
        e_mid = sb("b_e_mid", [P, B1])
        e_end = sb("b_e_end", [P, B1])
        e_q2 = sb("b_e_q2", [P, TB, CH])
        e_k1 = sb("b_e_k1", [P, TB, CH])
        q_all = sb("b_q_all", [P, B1])
        q_2 = sb("b_q_2", [P, TB, CH])
        k_1 = sb("b_k_1", [P, TB, P])
        k_mid = sb("b_k_mid", [P, B1])
        k_end = sb("b_k_end", [P, B1])
        dec = sb("b_dec", [P, TB])
        k_tok = sb("b_k_tok", [P, DK])
        att = sb("b_att", [P, P])
        state = sb("b_state", [P, DV])
        squares = sb("b_squares", [P, DV])
        ms = sb("b_ms", [P, 1])
        mse = sb("b_mse", [P, 1])
        rstd = sb("b_rstd", [P, 1])
        neg_half = sb("b_neg_half", [P, 1])
        o_n = sb("b_o_n", [P, DV])
        norm_col = sb("b_norm_col", [P, 2])
        y = sb("b_y", [P, 2, B1])

        h_loaded = [sem(f"b_h_loaded{i}") for i in range(2)]
        h_hi = sem("b_h_hi"); h_ready = sem("b_h_ready")
        gate_loaded = sem("b_gate_loaded"); w2_ready = sem("b_w2_ready"); gates_done = sem("b_gates_done")
        xg_ready = sem("b_xg_ready"); soft_step = sem("b_soft_step"); loga_ready = sem("b_loga_ready")
        sums_ready = sem("b_sums_ready")
        raw_loaded = [sem(f"b_raw_loaded{i}") for i in range(2)]
        passed = sem("b_passed")
        norm_loaded = sem("b_norm_loaded"); cols_loaded = sem("b_cols_loaded"); consts_ready = sem("b_consts")
        w_hi = sem("b_w_hi"); w_ready = sem("b_w_ready"); unit_done = sem("b_unit_done"); unit_out = sem("b_unit_out")
        gsilu = sem("b_gsilu"); q2_ready = sem("b_q2_ready"); d_ready = sem("b_d_ready"); exps_ready = sem("b_exps_ready"); prod_ready = sem("b_prod_ready")
        kt_done = sem("b_kt_done"); kt_ready = sem("b_kt_ready"); att_done = sem("b_att_done"); att_ready = sem("b_att_ready")
        o_done = sem("b_o_done"); kv_done = sem("b_kv_done"); state_ready = sem("b_state_ready")
        ms_ready = sem("b_ms_ready"); mse_ready = sem("b_mse_ready"); rstd_ready = sem("b_rstd_ready")
        on_ready = sem("b_on_ready"); ot_done = sem("b_ot_done"); y_ready = sem("b_y_ready"); y_stored = sem("b_y_stored")

        STEPS = GH * NB

        H_SLOTS = (5, 6, 8, 10)
        W_SLOTS = tuple(2 * u + 3 for u in range(UV))
        V_SLOTS = (1, 3)

        def part(u, p):
            return w[:, u, :, p, :] if u < UV else w_v[:, :, p, (u - UV) * P:(u - UV + 1) * P]

        def column(h, u):
            return (CQ + h * DK, CK + h * DK, CG + h * DV, CG + h * DV + P, CV + h * DV, CV + h * DV + P)[u]

        with nc.Block() as block:
            @block.sync
            def _(sp):
                def load_w(h, u):
                    wait(sp, w_ready, h * U + u - 1)
                    sp.dma_start(w_raw[:, u % 2], w_rows[:, :, bass.ds(column(h, u), P)]).then_inc(raw_loaded[u % 2], 16)

                def load_h(n, s, q):
                    wait(sp, h_ready, n * QS + q - 1)
                    sp.dma_start(h_raw[:, q % 2], h_d[s, :, q * QK:(q + 1) * QK, :]).then_inc(h_loaded[q % 2], 16)

                def store_y(n, h, s):
                    sp.wait_ge(y_ready, n * TB + TB)
                    for b in range(B1 // B2):
                        sp.dma_start(y_d[s * (B1 // B2) + b, :, bass.ds(h * 2, 2), :],
                                     y[:, :, b * B2:(b + 1) * B2]).then_inc(y_stored, 16)

                for u in range(U):
                    load_w(0, u)
                    if u < QS:
                        load_h(0, 0, u)

                def head(h, last):
                    for s in range(NB):
                        n = h * NB + s
                        if s < NB - 1 or not last:
                            for q in range(QS):
                                load_h(n + 1, (s + 1) % NB, q)
                                if s == NB - 1:
                                    for u in ((0, 1), (), (2,), (3, 4, 5))[q]:
                                        load_w(h + 1, u)
                        if s > 0:
                            store_y(n - 1, h, s - 1)
                        elif not isinstance(h, int) or h > 0:
                            store_y(n - 1, h - 1, NB - 1)

                head(0, False)
                with sp.Fori(1, GH - 1) as h:
                    head(h, False)
                head(GH - 1, True)
                store_y(STEPS - 1, GH - 1, NB - 1)
                sp.wait_ge(y_stored, 32 * STEPS)

            @block.gpsimd
            def _(pool):
                pool.memset(k_1[:, :, :], 0.0).then_inc(consts_ready, 1)
                pool.memset(att[:, :], 0.0).then_inc(consts_ready, 1)
                pool.memset(neg_half[:, :], -0.5).then_inc(consts_ready, 1)
                pool.wait_ge(consts_ready, 3)
                pool.dma_start(w2[:, :], gla_gate_w2[0]).then_inc(gate_loaded, 16)
                pool.dma_start(gb[:, :], gla_gate_b[0].rearrange("(h p) -> p h", p=P), allow_slow_non_contiguous=True).then_inc(gate_loaded, 16)
                pool.dma_start(norm_col[:, :], gla_norm_w[0].rearrange("(k p) -> p k", p=P), allow_slow_non_contiguous=True).then_inc(norm_loaded, 16)

                def rstd_of(r, t):
                    m = r * TB + t
                    pool.wait_ge(ms_ready, m + 1)
                    pool.sem_inc(passed, 1)
                    pool.tensor_scalar(mse[:, :], ms[:, :], EPS, None, ALU.add).then_inc(mse_ready, 1)
                    pool.wait_ge(mse_ready, m + 1)
                    wait(pool, on_ready, m)
                    pool.tensor_tensor(rstd[:, :], mse[:, :], neg_half[:, :], ALU.pow).then_inc(rstd_ready, 1)

                for t in range(TAPS):
                    pool.dma_start(conv_col[:, t, :], conv_w[0, t].rearrange("(k p) -> p k", p=P), allow_slow_non_contiguous=True).then_inc(cols_loaded, 16)
                pool.dma_start(convb_col[:, :], conv_b[0].rearrange("(k p) -> p k", p=P), allow_slow_non_contiguous=True).then_inc(cols_loaded, 16)
                for i in range(P // SP_):
                    pool.dma_start(d_col[i * SP_:(i + 1) * SP_, :],
                                   d_skip[0].rearrange("(k i) -> i k", i=P // SP_)[i].partition_broadcast(SP_)
                                   , allow_slow_non_contiguous=True).then_inc(cols_loaded, 16)
                pool.dma_start(ssd_norm_col[:, :], ssd_norm_w[0].rearrange("(k p) -> p k", p=P), allow_slow_non_contiguous=True).then_inc(cols_loaded, 16)

                for t in range(TB):
                    rstd_of(0, t)
                with pool.Fori(1, STEPS) as r:
                    for t in range(TB):
                        rstd_of(r, t)
                pool.wait_ge(cols_loaded, 16 * (TAPS + 4))

            @block.scalar
            def _(act):
                def w_high(h, u):
                    act.wait_ge(raw_loaded[u % 2], (h * (U // 2) + u // 2 + 1) * 16)
                    wait(act, unit_done, (h * NB - 1) * U + (u + 1 if u < UV else U))
                    act.activation(part(u, HI), w_raw[:, u % 2], ACT.Copy).then_inc(w_hi, 1)

                def h_high(n, q, par):
                    act.wait_ge(h_loaded[q % 2], (n * (QS // 2) + q // 2 + 1) * 16)
                    wait(act, unit_done, (n - 1) * U)
                    act.activation(hl[:, par, q * QK:(q + 1) * QK, HI, :], h_raw[:, q % 2], ACT.Copy).then_inc(h_hi, 1)

                def soft_gate(n):
                    act.wait_ge(gates_done, n + 1)
                    wait(act, loga_ready, n)
                    act.activation(xg[:, :], ps[:, GATE, :], ACT.Identity, bias=gb_h[:, :]).then_inc(xg_ready, 1)
                    act.wait_ge(xg_ready, n + 1)
                    act.activation(soft[:, :], xg[:, :], ACT.Abs).then_inc(soft_step, 1)
                    act.wait_ge(soft_step, n * 3 + 1)
                    act.activation(soft[:, :], soft[:, :], ACT.Exp, scale=-1.0).then_inc(soft_step, 1)
                    act.wait_ge(soft_step, n * 3 + 2)
                    act.activation(soft[:, :], soft[:, :], ACT.Ln, bias=1.0).then_inc(soft_step, 1)

                def evacuate(n, u, par):
                    act.wait_ge(unit_done, n * U + u + 1)
                    if u in (UQ, UK):
                        wait(act, prod_ready, n)
                        dst = qk[:, u - UQ, :]
                    elif u in (UG, UG + 1):
                        wait(act, y_ready, (n - 1) * TB)
                        dst = gz[:, par, u - UG, :]
                    else:
                        wait(act, kv_done, (n - 1) * TB)
                        dst = v[:, par, (u - UV) * 2:(u - UV) * 2 + 2, :].rearrange("p t n -> p (t n)")
                    act.activation(dst, ps[:, PROJ + u % 2, :], ACT.Copy).then_inc(unit_out, 1)

                def exps(n):
                    act.wait_ge(d_ready, n + 1)
                    cb = sums[:, :].rearrange("p (t n) -> p t n", n=P)
                    act.activation(e_k1[:, :, :], cb[:, :, 0:CH], ACT.Exp, scale=-1.0 / TAU)
                    act.activation(e_all[:, :], sums[:, :], ACT.Exp, scale=1.0 / TAU)
                    mid = e_mid[:, :].rearrange("p (t n) -> p t n", n=P)
                    act.activation(e_q2[:, :, :], mid[:, :, CH:P], ACT.Exp, scale=-1.0 / TAU).then_inc(q2_ready, 1)
                    act.wait_ge(q2_ready, n + 1)
                    act.activation(e_mid[:, :], e_mid[:, :], ACT.Exp, scale=1.0 / TAU)
                    act.activation(e_end[:, :], e_end[:, :], ACT.Exp, scale=1.0 / TAU).then_inc(exps_ready, 1)

                def silu_gate(n, par):
                    act.wait_ge(unit_out, n * U + UG + 2)
                    act.activation(gz[:, par], gz[:, par], ACT.Silu).then_inc(gsilu, 1)

                def kt_copy(r, t):
                    m = r * TB + t
                    act.wait_ge(kt_done, m + 1)
                    wait(act, kv_done, m)
                    act.activation(k_tok[:, :], ps[:, KTURN, 0:DK], ACT.Copy).then_inc(kt_ready, 1)

                def normed(r, t):
                    m = r * TB + t
                    act.wait_ge(o_done, m + 1)
                    wait(act, mse_ready, m)
                    wait(act, ms_ready, m)
                    act.activation(squares[:, :], ps[:, O, 0:DV], ACT.Square, scale=1.0 / 16.0,
                                   accum_out=ms[:, :]).then_inc(ms_ready, 1)
                    act.wait_ge(rstd_ready, m + 1)
                    wait(act, ot_done, m)
                    act.activation(o_n[:, :], ps[:, O, 0:DV], ACT.Copy, scale=rstd[:, :]).then_inc(on_ready, 1)

                def step(n, h, s, first, last):
                    par = s % 2
                    for i in range(3 * TB):
                        if i % 2 == 1:
                            evacuate(n, i // 2, par)
                        if not first and i % 3 == 0:
                            kt_copy(n - 1, i // 3)
                        if i == 0:
                            soft_gate(n)
                        if not first and i % 3 == 1:
                            normed(n - 1, i // 3)
                        if i in V_SLOTS and s == 0 and not first:
                            w_high(h, UV + V_SLOTS.index(i))
                        if i == 2:
                            exps(n)
                        if i == 7:
                            silu_gate(n, par)
                        if i in H_SLOTS and not last:
                            h_high(n + 1, H_SLOTS.index(i), 1 - par)
                        if i in W_SLOTS and s == NB - 1 and not last:
                            w_high(h + 1, W_SLOTS.index(i))

                for u in range(U):
                    w_high(0, u)
                    if u < QS:
                        h_high(0, u, 0)
                step(0, 0, 0, True, False)
                for s in range(1, NB):
                    step(s, 0, s, False, False)
                with act.Fori(1, GH - 1) as h:
                    for s in range(NB):
                        step(h * NB + s, h, s, False, False)
                for s in range(NB):
                    step(STEPS - NB + s, GH - 1, s, False, s == NB - 1)
                kt_copy(STEPS - 1, 0)
                for t in range(TB):
                    if t < TB - 1:
                        kt_copy(STEPS - 1, t + 1)
                    normed(STEPS - 1, t)

            @block.vector
            def _(dve):

                def w_low(h, u):
                    dve.wait_ge(w_hi, h * U + u + 1)
                    dve.tensor_tensor(part(u, LO), w_raw[:, u % 2], part(u, HI).bitcast(F32),
                                      ALU.subtract).then_inc(w_ready, 1)

                def h_low(n, q, par):
                    dve.wait_ge(h_hi, n * QS + q + 1)
                    ks = slice(q * QK, (q + 1) * QK)
                    dve.tensor_tensor(hl[:, par, ks, LO, :], h_raw[:, q % 2], hl[:, par, ks, HI, :].bitcast(F32),
                                      ALU.subtract).then_inc(h_ready, 1)

                def head_gate(h):
                    wait(dve, gates_done, h * NB)
                    wait(dve, xg_ready, h * NB)
                    dve.tensor_copy(w2_h[:, :], w2[:, bass.ds(h * DK, DK)]).then_inc(w2_ready, 1)
                    dve.tensor_copy(gb_h[:, :], gb[:, bass.ds(h, 1)]).then_inc(w2_ready, 1)

                def gate_sums(n):
                    dve.wait_ge(soft_step, n * 3 + 3)
                    dve.scalar_tensor_tensor(out=xg[:, :], in0=xg[:, :], scalar=0.0, in1=soft[:, :],
                                             op0=ALU.min, op1=ALU.subtract).then_inc(loga_ready, 1)
                    dve.wait_ge(loga_ready, n + 1)
                    wait(dve, exps_ready, n)
                    dve.tensor_tensor_scan(sums[:, :], keep_row[:, :], xg[:, :], 0.0, ALU.mult,
                                           ALU.add).then_inc(sums_ready, 1)

                def differences(n):
                    dve.wait_ge(sums_ready, n + 1)
                    wait(dve, prod_ready, n)
                    cb = sums[:, :].rearrange("p (t n) -> p t n", n=P)
                    dve.tensor_tensor(e_mid[:, :].rearrange("p (t n) -> p t n", n=P),
                                      cb[:, :, CH - 1:CH].broadcast_to([P, TB, P]), cb, ALU.subtract)
                    dve.tensor_tensor(e_end[:, :].rearrange("p (t n) -> p t n", n=P),
                                      cb[:, :, P - 1:P].broadcast_to([P, TB, P]), cb, ALU.subtract).then_inc(d_ready, 1)

                def products(n):
                    dve.wait_ge(unit_out, n * U + UK + 1)
                    dve.wait_ge(exps_ready, n + 1)
                    wait(dve, kv_done, n * TB)
                    wait(dve, state_ready, n * TB)
                    q3, k3 = (qk[:, i, :].rearrange("p (t n) -> p t n", n=P) for i in range(2))
                    scale = DK ** -0.5
                    dve.scalar_tensor_tensor(out=q_all[:, :], in0=qk[:, 0, :], scalar=scale, in1=e_all[:, :],
                                             op0=ALU.mult, op1=ALU.mult)
                    dve.scalar_tensor_tensor(out=q_2[:, :, :], in0=q3[:, :, CH:P], scalar=scale, in1=e_q2[:, :, :],
                                             op0=ALU.mult, op1=ALU.mult)
                    dve.tensor_tensor(k_1[:, :, 0:CH], k3[:, :, 0:CH], e_k1[:, :, :], ALU.mult)
                    dve.tensor_tensor(k_mid[:, :], qk[:, 1, :], e_mid[:, :], ALU.mult)
                    dve.tensor_tensor(k_end[:, :], qk[:, 1, :], e_end[:, :], ALU.mult)
                    dve.tensor_copy(dec[:, :], e_all[:, :].rearrange("p (t n) -> p t n", n=P)[:, :, P - 1]).then_inc(prod_ready, 1)

                def mask_att(r, t):
                    m = r * TB + t
                    dve.wait_ge(att_done, m + 1)
                    wait(dve, o_done, m)
                    dve.sem_inc(passed, 1)
                    dve.copy_predicated(att[:, :], causal[:, :].bitcast(I32), ps[:, AT, 0:P]).then_inc(att_ready, 1)

                def update_state(r, t, fresh):
                    m = r * TB + t
                    dve.wait_ge(kv_done, m + 1)
                    dve.wait_ge(prod_ready, r + 1)
                    if fresh:
                        dve.tensor_copy(state[:, :], ps[:, KV, 0:DV]).then_inc(state_ready, 1)
                    else:
                        dve.wait_ge(state_ready, m)
                        dve.scalar_tensor_tensor(out=state[:, :], in0=state[:, :], scalar=dec[:, t:t + 1],
                                                 in1=ps[:, KV, 0:DV], op0=ALU.mult, op1=ALU.add).then_inc(state_ready, 1)

                def gated(r, t, par):
                    m = r * TB + t
                    dve.wait_ge(ot_done, m + 1)
                    if t == 0:
                        dve.wait_ge(gsilu, r + 1)
                        wait(dve, y_stored, r * 32)
                    for f in range(2):
                        last = dve.scalar_tensor_tensor(
                            out=y[:, f, t * P:(t + 1) * P], in0=ps[:, OT, f * P:(f + 1) * P], scalar=norm_col[:, f:f + 1],
                            in1=gz[:, par, f, t * P:(t + 1) * P], op0=ALU.mult, op1=ALU.mult)
                    last.then_inc(y_ready, 1)

                def step(n, h, s, first, last):
                    fresh = (s - 1) % NB == 0
                    for i in range(3 * TB):
                        t = i // 3
                        if i == 3 * TB - 1:
                            products(n)
                        if i % 3 == 0 and not first:
                            mask_att(n - 1, t)
                        if i % 3 == 1 and not first:
                            update_state(n - 1, t, fresh and t == 0)
                        if i % 3 == 2 and not first:
                            gated(n - 1, t, (s - 1) % 2)
                        if i == 0:
                            gate_sums(n)
                            differences(n)
                        if i in V_SLOTS and s == 0 and not first:
                            w_low(h, UV + V_SLOTS.index(i))
                        if i == 9 and s == NB - 1 and not last:
                            head_gate(h + 1)
                        if i in H_SLOTS and not last:
                            h_low(n + 1, H_SLOTS.index(i), (s + 1) % 2)
                        if i in W_SLOTS and s == NB - 1 and not last:
                            w_low(h + 1, W_SLOTS.index(i))

                for u in range(U):
                    w_low(0, u)
                    if u < QS:
                        h_low(0, u, 0)
                dve.wait_ge(consts_ready, 3)
                dve.wait_ge(norm_loaded, 16)
                dve.wait_ge(gate_loaded, 32)
                head_gate(0)
                step(0, 0, 0, True, False)
                for s in range(1, NB):
                    step(s, 0, s, False, False)
                with dve.Fori(1, GH - 1) as h:
                    for s in range(NB):
                        step(h * NB + s, h, s, False, False)
                for s in range(NB):
                    step(STEPS - NB + s, GH - 1, s, False, s == NB - 1)
                mask_att(STEPS - 1, 0)
                for t in range(TB):
                    if t < TB - 1:
                        mask_att(STEPS - 1, t + 1)
                    update_state(STEPS - 1, t, False)
                    if t > 0:
                        gated(STEPS - 1, t - 1, (NB - 1) % 2)
                gated(STEPS - 1, TB - 1, (NB - 1) % 2)

            @block.tensor
            def _(pe):
                def half_unit(n, h, u, half, par):
                    if half == 0:
                        pe.wait_ge(w_ready, h * U + (u + 1 if u < UV else U))
                        wait(pe, unit_out, n * U + u - 1)
                    if u < UV:
                        for k in range(half * KT // 2, (half + 1) * KT // 2):
                            if u == 0 and k % QK == 0:
                                pe.wait_ge(h_ready, n * QS + k // QK + 1)
                            for i, (a, b) in enumerate(PASSES):
                                mm = pe.matmul(ps[:, PROJ + u % 2, :], w[:, u, k, a, :], hl[:, par, k, b, :],
                                               start=(k == 0 and i == 0), stop=(k == KT - 1 and i == 2))
                    else:
                        t = (u - UV) * 2 + half
                        for k in range(KT):
                            for i, (a, b) in enumerate(PASSES):
                                mm = pe.matmul(ps[:, PROJ + u % 2, half * DV:(half + 1) * DV],
                                               hl[:, par, k, a, t * P:(t + 1) * P], w_v[:, k, b, :],
                                               start=(k == 0 and i == 0), stop=(k == KT - 1 and i == 2))
                    if half == 1:
                        mm.then_inc(unit_done, 1)

                def scores(r, t):
                    m = r * TB + t
                    if t == 0:
                        pe.wait_ge(prod_ready, r + 1)
                    wait(pe, kt_ready, m)
                    cols = slice(t * P, (t + 1) * P)
                    pe.transpose(ps[:, KTURN, 0:DK], k_end[:, cols], ident[:, :]).then_inc(kt_done, 1)
                    wait(pe, att_ready, m)
                    pe.matmul(ps[:, AT, 0:CH], k_1[:, t, :], q_all[:, t * P:t * P + CH], start=True, stop=True)
                    pe.matmul(ps[:, AT, CH:P], k_mid[:, cols], q_2[:, t, :], start=True, stop=True).then_inc(att_done, 1)

                def outputs(r, t, fresh, par):
                    m = r * TB + t
                    wait(pe, on_ready, m)
                    pe.wait_ge(att_ready, m + 1)
                    pe.wait_ge(kt_ready, m + 1)
                    if t == 0:
                        pe.wait_ge(unit_out, r * U + U)
                    mm = pe.matmul(ps[:, O, 0:DV], att[:, :], v[:, par, t, :], start=True, stop=fresh)
                    if not fresh:
                        pe.wait_ge(state_ready, m)
                        mm = pe.matmul(ps[:, O, 0:DV], q_all[:, t * P:(t + 1) * P], state[:, :], start=False, stop=True)
                    mm.then_inc(o_done, 1)
                    wait(pe, state_ready, m)
                    pe.matmul(ps[:, KV, 0:DV], k_tok[:, :], v[:, par, t, :], start=True, stop=True).then_inc(kv_done, 1)

                def turn(r, t):
                    m = r * TB + t
                    pe.wait_ge(on_ready, m + 1)
                    wait(pe, y_ready, m)
                    for f in range(2):
                        mm = pe.transpose(ps[:, OT, f * P:(f + 1) * P], o_n[:, f * P:(f + 1) * P], ident[:, :])
                    mm.then_inc(ot_done, 1)

                def gates(n, h, s):
                    pe.wait_ge(w2_ready, h * 2 + 2)
                    wait(pe, xg_ready, n)
                    pe.matmul(ps[:, GATE, :], w2_h[:, :], code[:, s * B1:(s + 1) * B1], start=True,
                              stop=True).then_inc(gates_done, 1)

                def step(n, h, s, first):
                    par = s % 2
                    fresh = (s - 1) % NB == 0
                    for i in range(3 * TB):
                        t = i // 3
                        half_unit(n, h, i // 2, i % 2, par)
                        if i == (3 if first else 0):
                            gates(n, h, s)
                        if not first:
                            if i % 3 == 0:
                                scores(n - 1, t)
                            if i % 3 == 1:
                                outputs(n - 1, t, fresh and t == 0, 1 - par)
                            if i % 3 == 2:
                                turn(n - 1, t)

                step(0, 0, 0, True)
                for s in range(1, NB):
                    step(s, 0, s, False)
                with pe.Fori(1, GH) as h:
                    for s in range(NB):
                        step(h * NB + s, h, s, False)
                scores(STEPS - 1, 0)
                for t in range(TB):
                    if t < TB - 1:
                        scores(STEPS - 1, t + 1)
                    outputs(STEPS - 1, t, False, (NB - 1) % 2)
                    if t > 0:
                        turn(STEPS - 1, t - 1)
                turn(STEPS - 1, TB - 1)


def ssd(nc, w_rows, conv_col, convb_col, d_col, norm_col, ps, ident, tok, h_d, ac_d, y_d, T, KT, G, HG, GW, XT, NS,
        SP_, INNER, VAL, TAPS, CZ, CX, B2, TB2):
    UB, UC, UX, UZ = 0, 1, 2, 2 + XT
    UCONV, U = UZ, UZ + XT
    S = T // B2
    HIST = TAPS - 1
    PROJ, X, BC, Y, YI, ST, YT = 0, 2, 3, 4, 5, 6, 7
    QS = 4
    QK = KT // QS
    with ExitStack() as ctx:
        def sb(name, shape, dt=F32):
            return ctx.enter_context(nc.sbuf_tensor(name, shape, dt))

        def sem(name):
            return ctx.enter_context(nc.semaphore(name))

        hl = sb("c_hl", [P, 2, KT, 2, B2], F32R)
        w = sb("c_w", [P, U, KT, 2, P], F32R)
        w_raw = sb("c_w_raw", [P, 2, KT, P])
        h_raw = sb("c_h_raw", [P, 2, QK, B2])
        past = sb("c_past", [P, P])
        mean = sb("c_mean", [P, P])
        eps = sb("c_eps", [P, 1])
        before = sb("c_before", [P, UCONV, HIST + B2])
        acc = sb("c_acc", [P, UCONV, B2])
        xbc = sb("c_xbc", [P, 2, UCONV, B2])
        z = sb("c_z", [P, 2, XT, B2])
        ac = sb("c_ac", [P, HG, B2])
        decay = sb("c_decay", [P, HG, B2])
        chunk = sb("c_chunk", [P, HG, TB2])
        wt = sb("c_wt", [P, HG, P])
        xdt = sb("c_xdt", [P, HG, SP_])
        xend = sb("c_xend", [P, HG, SP_])
        btok = sb("c_btok", [P, NS])
        state = sb("c_state", [P, HG, SP_])
        decayed = sb("c_decayed", [P, HG, SP_])
        yi = sb("c_yi", [P, HG, SP_])
        yt = sb("c_yt", [P, GW])
        gated = sb("c_gated", [P, XT, B2])
        sq = sb("c_sq", [P, XT, B2])
        root = sb("c_root", [P, B2])
        rstd = root
        y = sq

        h_loaded = [sem(f"c_h_loaded{i}") for i in range(2)]
        h_hi = sem("c_h_hi"); h_ready = sem("c_h_ready")
        raw_loaded = [sem(f"c_raw_loaded{i}") for i in range(2)]
        passed = sem("c_passed")
        ac_loaded = sem("c_ac_loaded"); consts_ready = sem("c_consts")
        w_hi = sem("c_w_hi"); w_ready = sem("c_w_ready"); unit_done = sem("c_unit_done"); unit_out = sem("c_unit_out")
        tap_ready = sem("c_tap_ready"); conv_step = sem("c_conv_step"); conv_ready = sem("c_conv_ready")
        hist_ready = sem("c_hist_ready"); xbc_ready = sem("c_xbc_ready")
        seg_ready = sem("c_seg_ready"); decay_ready = sem("c_decay_ready")
        x_done = sem("c_x_done"); bc_done = sem("c_bc_done"); xdt_ready = sem("c_xdt_ready"); xend_ready = sem("c_xend_ready")
        wt_ready = sem("c_wt_ready"); y_done = sem("c_y_done"); yi_done = sem("c_yi_done"); st_done = sem("c_st_done")
        yi_ready = sem("c_yi_ready"); yt_ready = sem("c_yt_ready"); decayed_ready = sem("c_decayed_ready")
        state_ready = sem("c_state_ready"); turned = sem("c_turned"); skip_ready = sem("c_skip_ready")
        gated_ready = sem("c_gated_ready"); sq_ready = sem("c_sq_ready"); mean_done = sem("c_mean_done")
        root_ready = sem("c_root_ready"); rstd_ready = sem("c_rstd_ready")
        y_ready = sem("c_y_ready"); y_stored = sem("c_y_stored")

        H_SLOTS = (1, 3, 5, 7)

        def column(g, u):
            if u < UX:
                return CX + INNER + (u - UB) * G * NS + g * NS
            return CX + g * GW + (u - UX) * P if u < UZ else CZ + g * GW + (u - UZ) * P

        def channel(g, u):
            return INNER // P + (u - UB) * G + g if u < UX else g * XT + u - UX

        with nc.Block() as block:
            @block.sync
            def _(sp):
                def load_w(g, u):
                    wait(sp, w_ready, g * U + u - 1)
                    sp.dma_start(w_raw[:, u % 2], w_rows[:, :, column(g, u):column(g, u) + P]).then_inc(raw_loaded[u % 2], 16)

                def load_h(n, b, par, q):
                    wait(sp, h_ready, n * QS + q - 1)
                    src = h_d[bass.ds((b - par) // 2, 1)] if isinstance(b, int) else h_d[bass.ds(b // 2, 1)]
                    sp.dma_start(h_raw[:, q % 2], src[:, :, q * QK:(q + 1) * QK, par * B2:(par + 1) * B2]
                                 .rearrange("a p k n -> (a p) k n")).then_inc(h_loaded[q % 2], 16)

                def load_ac(n, g, b):
                    wait(sp, decay_ready, n)
                    sp.dma_start(ac[:, :, :], ac_d[g * HG:(g + 1) * HG, bass.ds(b * B2, B2)].partition_broadcast(P)
                                 ).then_inc(ac_loaded, 16)

                def store_y(r, g, b):
                    sp.wait_ge(y_ready, r + 1)
                    f = VAL // P + g * XT
                    sp.dma_start(y_d[bass.ds(b, 1), :, f:f + XT, :].rearrange("a p f n -> (a p) f n"),
                                 y[:, :, :]).then_inc(y_stored, 16)

                for u in range(U):
                    load_w(0, u)
                    if u < QS:
                        load_h(0, 0, 0, u)
                    if u == QS:
                        load_ac(0, 0, 0)

                def step(g, n, s, par, nxt):
                    if nxt is not None:
                        for q in range(QS):
                            load_h(n + 1, nxt[1], 1 - par, q)
                            if nxt[0] != g:
                                for u in ((), (0, 1, 2, 3), (4, 5), (6, 7, 8, 9))[q]:
                                    load_w(g + 1, u)
                    if nxt is not None:
                        load_ac(n + 1, *nxt)
                    if not (isinstance(s, int) and s == 0):
                        store_y(n - 1, g, s - 1)
                    elif g > 0:
                        store_y(n - 1, g - 1, S - 1)

                for g in range(G):
                    step(g, g * S, 0, 0, (g, 1))
                    step(g, g * S + 1, 1, 1, (g, 2))
                    with sp.Fori(1, S // 2 - 1) as i:
                        step(g, 2 * i + g * S, 2 * i, 0, (g, 2 * i + 1))
                        step(g, 2 * i + (g * S + 1), 2 * i + 1, 1, (g, 2 * i + 2))
                    step(g, g * S + S - 2, S - 2, 0, (g, S - 1))
                    step(g, g * S + S - 1, S - 1, 1, (g + 1, 0) if g < G - 1 else None)
                store_y(G * S - 1, G - 1, S - 1)
                sp.wait_ge(y_stored, 16 * G * S)

            @block.gpsimd
            def _(pool):
                pool.memset(past[:, :], 0.0).then_inc(consts_ready, 1)
                pool.memset(mean[:, :], 1.0 / GW).then_inc(consts_ready, 1)
                pool.memset(eps[:, :], EPS).then_inc(consts_ready, 1)
                pool.memset(before[:, :, 0:HIST], 0.0).then_inc(consts_ready, 1)
                pool.wait_ge(consts_ready, 4)
                pool.affine_select(out=past[:, :], in_=past[:, :], compare_op=ALU.is_ge, fill=-1e30,
                                   base=0, pattern=[[1, P]], channel_multiplier=-1).then_inc(consts_ready, 1)

                def ends(r, g, b, t):
                    m = r * TB2 + t
                    pool.wait_ge(xdt_ready, m + 1)
                    wait(pool, st_done, m)
                    end = tok[:, bass.ds(b * TB2 + t, 1), 3, g * HG:(g + 1) * HG].rearrange("p a h -> p (a h)")
                    pool.tensor_tensor(xend[:, :, :], xdt[:, :, :], end.unsqueeze(2).broadcast_to([P, HG, SP_]),
                                       ALU.mult).then_inc(xend_ready, 1)

                def decay_state(r, g, t):
                    m = r * TB2 + t
                    pool.wait_ge(decay_ready, r + 1)
                    pool.wait_ge(state_ready, m + g + 1)
                    pool.tensor_tensor(decayed[:, :, :], state[:, :, :], chunk[:, :, t:t + 1].broadcast_to([P, HG, SP_]),
                                       ALU.mult).then_inc(decayed_ready, 1)

                def step(r, g, b):
                    for t in range(TB2):
                        ends(r, g, b, t)
                        decay_state(r, g, t)

                for g in range(G):
                    step(g * S, g, 0)
                    with pool.Fori(1, S) as i:
                        step(i + g * S, g, i)

            @block.scalar
            def _(act):

                def w_high(g, u):
                    act.wait_ge(raw_loaded[u % 2], (g * (U // 2) + u // 2 + 1) * 16)
                    wait(act, unit_done, (g * S - 1) * U + u + 1)
                    act.activation(w[:, u, :, HI, :], w_raw[:, u % 2], ACT.Copy).then_inc(w_hi, 1)

                def h_high(n, q, par):
                    act.wait_ge(h_loaded[q % 2], (n * (QS // 2) + q // 2 + 1) * 16)
                    wait(act, unit_done, (n - 1) * U)
                    act.activation(hl[:, par, q * QK:(q + 1) * QK, HI, :], h_raw[:, q % 2], ACT.Copy).then_inc(h_hi, 1)

                def evacuate(n, g, u, par):
                    act.wait_ge(unit_done, n * U + u + 1)
                    if u < UCONV:
                        wait(act, hist_ready, n)
                        ch = channel(g, u)
                        act.activation(before[:, u, HIST:], ps[:, PROJ + u % 2, 0:B2], ACT.Copy)
                        wait(act, xbc_ready, n)
                        act.activation(acc[:, u, :], ps[:, PROJ + u % 2, 0:B2], ACT.Identity,
                                       scale=conv_col[:, HIST, ch:ch + 1], bias=convb_col[:, ch:ch + 1]
                                       ).then_inc(unit_out, 1)
                    else:
                        wait(act, gated_ready, (n - 1) * TB2)
                        act.activation(z[:, par, u - UZ, :], ps[:, PROJ + u % 2, 0:B2], ACT.Silu).then_inc(unit_out, 1)

                def silu_conv(n, par):
                    act.wait_ge(conv_ready, n * UCONV + UCONV)
                    wait(act, gated_ready, (n - 1) * TB2)
                    act.activation(xbc[:, par], acc[:, :, :], ACT.Silu).then_inc(xbc_ready, 1)

                def decays(n):
                    act.wait_ge(seg_ready, n + 1)
                    wait(act, decayed_ready, n * TB2)
                    act.activation(chunk[:, :, :], ac[:, :, P - 1:B2:P], ACT.Exp)
                    act.activation(decay[:, :, :], decay[:, :, :], ACT.Exp).then_inc(decay_ready, 1)

                def squares(r):
                    act.wait_ge(gated_ready, (r + 1) * TB2)
                    wait(act, y_stored, r * 16)
                    act.activation(sq[:, :, :], gated[:, :, :], ACT.Square).then_inc(sq_ready, 1)

                def roots(r):
                    act.wait_ge(mean_done, r + 1)
                    wait(act, y_ready, r)
                    act.activation(root[:, :], ps[:, YT, 0:B2], ACT.Sqrt, bias=eps[:, :]).then_inc(root_ready, 1)

                def step(n, g, par, first, last, tail):
                    for u in range(U):
                        if u == UZ + 1 and not tail:
                            silu_conv(n, par)
                        if u == U - 1 and not first:
                            squares(n - 1)
                        if not tail:
                            evacuate(n, g, u, par)
                            if last and g < G - 1:
                                w_high(g + 1, u)
                            if u in H_SLOTS and not (last and g == G - 1):
                                h_high(n + 1, H_SLOTS.index(u), 1 - par)
                    if not first:
                        roots(n - 1)
                    if not tail:
                        decays(n)

                for u in range(U):
                    w_high(0, u)
                    if u < QS:
                        h_high(0, u, 0)
                act.wait_ge(consts_ready, 5)
                for g in range(G):
                    for s in range(2):
                        step(g * S + s, g, s, g == 0 and s == 0, False, False)
                    with act.Fori(1, S // 2 - 1) as i:
                        for s in range(2):
                            step(2 * i + (g * S + s), g, s, False, False, False)
                    for s in range(2):
                        step(g * S + S - 2 + s, g, s, False, s == 1, False)
                step(G * S, G, 0, False, True, True)

            @block.vector
            def _(dve):
                def w_low(g, u):
                    dve.wait_ge(w_hi, g * U + u + 1)
                    dve.tensor_tensor(w[:, u, :, LO, :], w_raw[:, u % 2], w[:, u, :, HI, :].bitcast(F32),
                                      ALU.subtract).then_inc(w_ready, 1)

                def h_low(n, q, par):
                    dve.wait_ge(h_hi, n * QS + q + 1)
                    ks = slice(q * QK, (q + 1) * QK)
                    dve.tensor_tensor(hl[:, par, ks, LO, :], h_raw[:, q % 2], hl[:, par, ks, HI, :].bitcast(F32),
                                      ALU.subtract).then_inc(h_ready, 1)

                def per_head(b, t, q, g):
                    cols = tok[:, bass.ds(b * TB2 + t, 1), q, g * HG:(g + 1) * HG].rearrange("p a h -> p (a h)")
                    return cols.unsqueeze(2).broadcast_to([P, HG, SP_])

                def bank(b):
                    return ps[:, b, :].rearrange("p (h w) -> p h w", w=SP_)

                def convolve(n, g, u):
                    dve.wait_ge(unit_out, n * U + u + 1)
                    ch = channel(g, u)
                    for k in range(HIST):
                        op = dve.scalar_tensor_tensor(out=acc[:, u, :], in0=before[:, u, k:k + B2],
                                                      scalar=conv_col[:, k, ch:ch + 1], in1=acc[:, u, :],
                                                      op0=ALU.mult, op1=ALU.add)
                        if k < HIST - 1:
                            op.then_inc(conv_step, 1)
                            dve.wait_ge(conv_step, (n * UCONV + u) * (HIST - 1) + k + 1)
                    op.then_inc(conv_ready, 1)

                def history(n, s_last):
                    dve.wait_ge(conv_ready, n * UCONV + UCONV)
                    if s_last:
                        dve.memset(before[:, :, 0:HIST], 0.0).then_inc(hist_ready, 1)
                    else:
                        dve.tensor_copy(before[:, :, 0:HIST], before[:, :, B2:B2 + HIST]).then_inc(hist_ready, 1)

                def tile_in(r, g, b, t):
                    m = r * TB2 + t
                    dve.wait_ge(x_done, m + 1)
                    wait(dve, y_done, m)
                    wait(dve, xend_ready, m)
                    dve.tensor_tensor(xdt[:, :, :], bank(X), per_head(b, t, 0, g), ALU.mult).then_inc(xdt_ready, 1)
                    dve.wait_ge(bc_done, m + 1)
                    dve.wait_ge(decay_ready, r + 1)
                    dve.tensor_tensor(wt[:, :, :], ps[:, BC, NS:NS + P].unsqueeze(1).broadcast_to([P, HG, P]),
                                      decay[:, :, t * P:(t + 1) * P], ALU.mult)
                    wait(dve, st_done, m)
                    dve.tensor_copy(btok[:, :], ps[:, BC, 0:NS]).then_inc(wt_ready, 1)

                def clear_state(r):
                    wait(dve, yi_done, r * TB2)
                    wait(dve, decayed_ready, r * TB2)
                    dve.memset(state[:, :, :], 0.0).then_inc(state_ready, 1)

                def tile_out(r, g, b, t):
                    m = r * TB2 + t
                    dve.wait_ge(yi_done, m + 1)
                    dve.tensor_tensor(yi[:, :, :], bank(YI), per_head(b, t, 2, g), ALU.mult).then_inc(yi_ready, 1)
                    dve.wait_ge(y_done, m + 1)
                    wait(dve, turned, m)
                    dve.wait_ge(yi_ready, m + 1)
                    dve.tensor_tensor(yt[:, :].rearrange("p (h w) -> p h w", w=SP_), bank(Y), yi[:, :, :],
                                      ALU.add).then_inc(yt_ready, 1)
                    dve.wait_ge(st_done, m + 1)
                    dve.wait_ge(decayed_ready, m + 1)
                    dve.tensor_tensor(state[:, :, :], bank(ST), decayed[:, :, :], ALU.add).then_inc(state_ready, 1)

                def tile_gate(r, g, t, par):
                    m = r * TB2 + t
                    dve.wait_ge(turned, m + 1)
                    dve.wait_ge(unit_out, r * U + U)
                    if t == 0:
                        wait(dve, y_ready, r)
                        wait(dve, sq_ready, r)
                    cols = slice(t * P, (t + 1) * P)
                    for f in range(XT):
                        k = g * XT + f
                        last = dve.scalar_tensor_tensor(out=gated[:, f, cols], in0=xbc[:, par, UX + f, cols],
                                                        scalar=d_col[:, k:k + 1], in1=ps[:, YT, f * P:(f + 1) * P],
                                                        op0=ALU.mult, op1=ALU.add)
                    last.then_inc(skip_ready, 1)
                    dve.wait_ge(skip_ready, m + 1)
                    dve.tensor_tensor(gated[:, :, cols], gated[:, :, cols], z[:, par, :, cols],
                                      ALU.mult).then_inc(gated_ready, 1)

                def segments(n, g, b):
                    dve.wait_ge(ac_loaded, n * 16 + 16)
                    wait(dve, wt_ready, n * TB2)
                    for t in range(TB2):
                        for h in range(HG):
                            k = g * HG + h
                            own = tok[:, bass.ds(b * TB2 + t, 1), 1, k:k + 1].rearrange("p a h -> p (a h)")
                            last = dve.scalar_tensor_tensor(
                                out=decay[:, h, t * P:(t + 1) * P], in0=ac[:, h, t * P:(t + 1) * P], scalar=own,
                                in1=past[:, :], op0=ALU.subtract, op1=ALU.min)
                    last.then_inc(seg_ready, 1)

                def finish(r, g):
                    dve.wait_ge(root_ready, r + 1)
                    dve.reciprocal(rstd[:, :], root[:, :]).then_inc(rstd_ready, 1)
                    dve.wait_ge(rstd_ready, r + 1)
                    for f in range(XT):
                        k = g * XT + f
                        last = dve.scalar_tensor_tensor(out=y[:, f, :], in0=gated[:, f, :], scalar=norm_col[:, k:k + 1],
                                                        in1=rstd[:, :], op0=ALU.mult, op1=ALU.mult)
                    last.then_inc(y_ready, 1)

                def step(n, g, b, par, rg, rb, first_of_group, last_of_group):
                    going, back = g is not None, rg is not None
                    split_w = last_of_group and g < G - 1
                    if back and first_of_group:
                        clear_state(n - 1)
                    for u in range(U):
                        if back and u == 0:
                            tile_in(n - 1, rg, rb, 0)
                        if back and u == 2:
                            tile_out(n - 1, rg, rb, 0)
                        if back and u == 4:
                            tile_gate(n - 1, rg, 0, 1 - par)
                            tile_in(n - 1, rg, rb, 1)
                        if back and u == UZ:
                            tile_out(n - 1, rg, rb, 1)
                        if back and u == U - 2:
                            tile_gate(n - 1, rg, 1, 1 - par)
                        if going and u < UZ:
                            convolve(n, g, u)
                            if u == UZ - 1:
                                history(n, last_of_group)
                        if going and u == UZ:
                            segments(n, g, b)
                        if split_w and u < U - 1:
                            w_low(g + 1, u)
                        if going and u in H_SLOTS and not (last_of_group and g == G - 1):
                            h_low(n + 1, H_SLOTS.index(u), 1 - par)
                    if back:
                        finish(n - 1, rg)
                    if split_w:
                        w_low(g + 1, U - 1)

                for u in range(U):
                    w_low(0, u)
                    if u < QS:
                        h_low(0, u, 0)
                dve.wait_ge(consts_ready, 5)
                for g in range(G):
                    before_g = (g - 1, S - 1) if g > 0 else (None, None)
                    step(g * S, g, 0, 0, *before_g, False, False)
                    step(g * S + 1, g, 1, 1, g, 0, True, False)
                    with dve.Fori(1, S // 2 - 1) as i:
                        for s in range(2):
                            step(2 * i + (g * S + s), g, 2 * i + s, s, g, 2 * i + (s - 1), False, False)
                    step(g * S + S - 2, g, S - 2, 0, g, S - 3, False, False)
                    step(g * S + S - 1, g, S - 1, 1, g, S - 2, False, True)
                step(G * S, None, 0, 0, G - 1, S - 1, False, False)

            @block.tensor
            def _(pe):
                pe.wait_ge(consts_ready, 5)

                def unit(n, g, u, par):
                    pe.wait_ge(w_ready, g * U + u + 1)
                    wait(pe, unit_out, n * U + u - 1)
                    for k in range(KT):
                        if u == 0 and k % QK == 0:
                            pe.wait_ge(h_ready, n * QS + k // QK + 1)
                        for i, (a, b) in enumerate(PASSES):
                            mm = pe.matmul(ps[:, PROJ + u % 2, 0:B2], w[:, u, k, a, :], hl[:, par, k, b, :],
                                           start=(k == 0 and i == 0), stop=(k == KT - 1 and i == 2))
                    mm.then_inc(unit_done, 1)

                def tile_in(r, t, par):
                    m = r * TB2 + t
                    cols = slice(t * P, (t + 1) * P)
                    pe.wait_ge(xbc_ready, r + 1)
                    wait(pe, xdt_ready, m)
                    for f in range(XT):
                        mm = pe.transpose(ps[:, X, f * P:(f + 1) * P], xbc[:, par, UX + f, cols], ident[:, :])
                    mm.then_inc(x_done, 1)
                    wait(pe, wt_ready, m)
                    pe.transpose(ps[:, BC, 0:NS], xbc[:, par, UB, cols], ident[:, :])
                    pe.matmul(ps[:, BC, NS:NS + P], xbc[:, par, UB, cols], xbc[:, par, UC, cols], start=True,
                              stop=True).then_inc(bc_done, 1)

                def tile_out(r, g, t, par):
                    m = r * TB2 + t
                    pe.wait_ge(state_ready, m + g + 1)
                    wait(pe, yi_ready, m)
                    pe.matmul(ps[:, YI, :], xbc[:, par, UC, t * P:(t + 1) * P],
                              state[:, :, :].rearrange("p h w -> p (h w)"), start=True, stop=True).then_inc(yi_done, 1)
                    pe.wait_ge(wt_ready, m + 1)
                    pe.wait_ge(xdt_ready, m + 1)
                    wait(pe, yt_ready, m)
                    for h in range(HG):
                        mm = pe.matmul(ps[:, Y, h * SP_:(h + 1) * SP_], wt[:, h, :], xdt[:, h, :], start=True, stop=True)
                    mm.then_inc(y_done, 1)
                    pe.wait_ge(xend_ready, m + 1)
                    pe.matmul(ps[:, ST, :], btok[:, :], xend[:, :, :].rearrange("p h w -> p (h w)"), start=True,
                              stop=True).then_inc(st_done, 1)

                def turn(r, t):
                    m = r * TB2 + t
                    pe.wait_ge(yt_ready, m + 1)
                    wait(pe, skip_ready, m)
                    wait(pe, root_ready, r)
                    for f in range(XT):
                        mm = pe.transpose(ps[:, YT, f * P:(f + 1) * P], yt[:, f * P:(f + 1) * P], ident[:, :])
                    mm.then_inc(turned, 1)

                def mean_squares(r):
                    pe.wait_ge(sq_ready, r + 1)
                    pe.wait_ge(skip_ready, r * TB2 + TB2)
                    for f in range(XT):
                        mm = pe.matmul(ps[:, YT, 0:B2], mean[:, :], sq[:, f, :], start=(f == 0), stop=(f == XT - 1))
                    mm.then_inc(mean_done, 1)

                def step(n, g, par, rg):
                    for t in range(TB2):
                        if rg is not None:
                            tile_in(n - 1, t, 1 - par)
                        if g is not None:
                            unit(n, g, 4 * t, par)
                            unit(n, g, 4 * t + 1, par)
                        if rg is not None:
                            tile_out(n - 1, rg, t, 1 - par)
                        if g is not None:
                            unit(n, g, 4 * t + 2, par)
                            unit(n, g, 4 * t + 3, par)
                        if rg is not None:
                            turn(n - 1, t)
                    if g is not None:
                        unit(n, g, 8, par)
                    if g is not None:
                        unit(n, g, 9, par)
                    if rg is not None:
                        mean_squares(n - 1)

                for g in range(G):
                    step(g * S, g, 0, g - 1 if g > 0 else None)
                    step(g * S + 1, g, 1, g)
                    with pe.Fori(1, S // 2) as i:
                        for s in range(2):
                            step(2 * i + (g * S + s), g, s, g)
                step(G * S, None, 0, G - 1)


def project_out(nc, x, w_out, out, ps, gate_row, y_d, D, FT, NB2, B2, TB2):
    HALVES = D // 512
    FQ = FT // 4
    with ExitStack() as ctx:
        def sb(name, shape, dt=F32):
            return ctx.enter_context(nc.sbuf_tensor(name, shape, dt))

        def sem(name):
            return ctx.enter_context(nc.semaphore(name))

        w = sb("d_w", [P, FT, 2, D], F32R)
        w_raw = sb("d_w_raw", [P, 2, D])
        y_raw = sb("d_y_raw", [P, FT, B2])
        yh = sb("d_yh", [P, TB2, FT, 2, P], F32R)
        x_sb = sb("d_x", [P, TB2, D])
        squares = sb("d_squares", [P, D])
        scaled = sb("d_scaled", [P, D])
        ms = sb("d_ms", [P, 1])
        mse = sb("d_mse", [P, 1])
        rstd = sb("d_rstd", [P, 1])
        neg_half = sb("d_neg_half", [P, 1])
        raw_loaded = [sem(f"d_raw_loaded{i}") for i in range(2)]
        x_loaded = [sem(f"d_x_loaded{i}") for i in range(TB2)]
        passed = sem("d_passed")
        w_hi = sem("d_w_hi"); w_ready = sem("d_w_ready"); consts_ready = sem("d_consts")
        y_loaded = sem("d_y_loaded"); first_loaded = [sem(f"d_first_loaded{i}") for i in range(2)]
        first_hi = sem("d_first_hi"); first_ready = sem("d_first_ready"); y_hi = sem("d_y_hi"); y_ready = sem("d_y_ready"); mixed_done = sem("d_mixed_done")
        ms_ready = sem("d_ms_ready"); mse_ready = sem("d_mse_ready"); rstd_ready = sem("d_rstd_ready")
        scaled_ready = sem("d_scaled_ready"); sum_ready = sem("d_sum_ready"); stored = [sem(f"d_stored{i}") for i in range(TB2)]

        with nc.Block() as block:
            @block.sync
            def _(sp):
                def load_x(b, t):
                    wait(sp, stored[t], b * 16)
                    rows = x[0, bass.ds(b * B2 + t * P, P), :]
                    sp.dma_start(x_sb[:, t, :], rows).then_inc(x_loaded[t], 16)

                def load_first_y(i):
                    sp.dma_start(y_raw[:, i * FQ:(i + 1) * FQ, :], y_d[0, :, i * FQ:(i + 1) * FQ, :]).then_inc(first_loaded[i % 2], 16)

                def load_y(b):
                    if isinstance(b, int):
                        sp.wait_ge(first_ready, FT // FQ * TB2)
                    else:
                        sp.wait_ge(y_ready, (b - 1) * TB2)
                    sp.dma_start(y_raw[:, :, :], y_d[bass.ds(b, 1)].rearrange("a p f n -> (a p) f n")).then_inc(y_loaded, 16)

                def load_w(f):
                    wait(sp, w_ready, f - 1)
                    sp.dma_start(w_raw[:, f % 2, :], w_out[0, f * P:(f + 1) * P, :]).then_inc(raw_loaded[f % 2], 16)

                for f in range(FT):
                    load_w(f)
                    if f % FQ == 0:
                        load_first_y(f // FQ)
                for t in range(TB2):
                    load_x(0, t)

                def store(b, t):
                    sp.wait_ge(sum_ready, b * TB2 + t + 1)
                    sp.dma_start(out[0, bass.ds(b * B2 + t * P, P), :], x_sb[:, t, :]).then_inc(stored[t], 16)

                load_y(1)
                for t in range(TB2):
                    store(0, t)
                    load_x(1, t)
                with sp.Fori(1, NB2 - 1) as b:
                    load_y(b + 1)
                    for t in range(TB2):
                        store(b, t)
                        load_x(b + 1, t)
                for t in range(TB2):
                    store(NB2 - 1, t)
                for t in range(TB2):
                    sp.wait_ge(stored[t], 16 * NB2)

            @block.gpsimd
            def _(pool):
                pool.memset(neg_half[:, :], -0.5).then_inc(consts_ready, 1)
                pool.wait_ge(consts_ready, 1)

                def rstd_of(m):
                    pool.wait_ge(ms_ready, m + 1)
                    wait(pool, rstd_ready, m)
                    pool.sem_inc(passed, 1)
                    pool.tensor_scalar(mse[:, :], ms[:, :], EPS, None, ALU.add).then_inc(mse_ready, 1)
                    pool.wait_ge(mse_ready, m + 1)
                    wait(pool, scaled_ready, m)
                    pool.tensor_tensor(rstd[:, :], mse[:, :], neg_half[:, :], ALU.pow).then_inc(rstd_ready, 1)

                rstd_of(0)
                with pool.Fori(1, NB2 * TB2) as m:
                    rstd_of(m)

            @block.scalar
            def _(act):
                def split_first(i, t):
                    if t == 0:
                        act.wait_ge(first_loaded[i % 2], (i // 2 + 1) * 16)
                    fs = slice(i * FQ, (i + 1) * FQ)
                    act.activation(yh[:, t, fs, HI, :], y_raw[:, fs, t * P:(t + 1) * P], ACT.Copy).then_inc(first_hi, 1)

                def split_y(b, t):
                    if t == 0:
                        act.wait_ge(y_loaded, b * 16)
                    wait(act, mixed_done, b * TB2 + t - (TB2 - 1))
                    act.activation(yh[:, t, :, HI, :], y_raw[:, :, t * P:(t + 1) * P], ACT.Copy).then_inc(y_hi, 1)

                def square(m, t):
                    act.wait_ge(mixed_done, m + 1)
                    wait(act, mse_ready, m)
                    wait(act, ms_ready, m)
                    act.activation(squares[:, :], ps[:, 2 * t:2 * t + 2, :].rearrange("p a n -> p (a n)"), ACT.Square,
                                   scale=1.0 / 32.0, accum_out=ms[:, :]).then_inc(ms_ready, 1)

                for f in range(FT):
                    act.wait_ge(raw_loaded[f % 2], (f // 2 + 1) * 16)
                    act.activation(w[:, f, HI, :], w_raw[:, f % 2, :], ACT.Copy).then_inc(w_hi, 1)
                    if f % FQ == 0:
                        for t in range(TB2):
                            split_first(f // FQ, t)
                for t in range(TB2):
                    split_y(1, t)
                    square(t, t)
                with act.Fori(1, NB2 - 1) as b:
                    for t in range(TB2):
                        square(b * TB2 + t, t)
                        split_y(b + 1, t)
                for t in range(TB2):
                    square((NB2 - 1) * TB2 + t, t)

            @block.vector
            def _(dve):
                def split_first(i, t):
                    dve.wait_ge(first_hi, i * TB2 + t + 1)
                    fs = slice(i * FQ, (i + 1) * FQ)
                    dve.tensor_tensor(yh[:, t, fs, LO, :], y_raw[:, fs, t * P:(t + 1) * P],
                                      yh[:, t, fs, HI, :].bitcast(F32), ALU.subtract).then_inc(first_ready, 1)

                def split_y(b, t):
                    dve.wait_ge(y_hi, (b - 1) * TB2 + t + 1)
                    dve.tensor_tensor(yh[:, t, :, LO, :], y_raw[:, :, t * P:(t + 1) * P],
                                      yh[:, t, :, HI, :].bitcast(F32), ALU.subtract).then_inc(y_ready, 1)

                def finish(b, t):
                    m = b * TB2 + t
                    dve.wait_ge(rstd_ready, m + 1)
                    wait(dve, sum_ready, m)
                    dve.scalar_tensor_tensor(out=scaled[:, :], in0=ps[:, 2 * t:2 * t + 2, :].rearrange("p a n -> p (a n)"),
                                             scalar=rstd[:, :], in1=gate_row[:, :], op0=ALU.mult,
                                             op1=ALU.mult).then_inc(scaled_ready, 1)
                    dve.wait_ge(scaled_ready, m + 1)
                    dve.wait_ge(x_loaded[t], b * 16 + 16)
                    dve.tensor_tensor(x_sb[:, t, :], x_sb[:, t, :], scaled[:, :], ALU.add).then_inc(sum_ready, 1)

                for f in range(FT):
                    dve.wait_ge(w_hi, f + 1)
                    dve.tensor_tensor(w[:, f, LO, :], w_raw[:, f % 2, :], w[:, f, HI, :].bitcast(F32),
                                      ALU.subtract).then_inc(w_ready, 1)
                    if f % FQ == 0:
                        for t in range(TB2):
                            split_first(f // FQ, t)
                for t in range(TB2):
                    split_y(1, t)
                    finish(0, t)
                with dve.Fori(1, NB2 - 1) as b:
                    for t in range(TB2):
                        finish(b, t)
                        split_y(b + 1, t)
                for t in range(TB2):
                    finish(NB2 - 1, t)

            @block.tensor
            def _(pe):
                def products(t, f):
                    for i, (a, c) in enumerate(PASSES):
                        for j in range(HALVES):
                            mm = pe.matmul(ps[:, 2 * t + j, :], yh[:, t, f, a, :], w[:, f, c, j * 512:(j + 1) * 512],
                                           start=(f == 0 and i == 0), stop=(f == FT - 1 and i == 2))
                    if f == FT - 1:
                        mm.then_inc(mixed_done, 1)

                for i in range(FT // FQ):
                    for t in range(TB2):
                        pe.wait_ge(first_ready, i * TB2 + t + 1)
                        for f in range(i * FQ, (i + 1) * FQ):
                            if t == 0:
                                pe.wait_ge(w_ready, f + 1)
                            products(t, f)
                with pe.Fori(1, NB2) as b:
                    for t in range(TB2):
                        m = b * TB2 + t
                        pe.wait_ge(y_ready, m - TB2 + 1)
                        pe.wait_ge(scaled_ready, m - (TB2 - 1))
                        for f in range(FT):
                            products(t, f)


_INS = ["x", "c", "ada_w", "ada_b", "pre_norm_w", "w_in", "gla_gate_w2", "gla_gate_b", "gla_norm_w", "conv_w", "conv_b",
        "dt_bias", "a_log", "d_skip", "ssd_norm_w", "w_out", "post_norm_w"]


def kernel(**inputs):
    import numpy as np
    import concourse.bacc as bacc
    from concourse.bass_utils import run_bass_kernel_spmd

    nc = bacc.Bacc("TRN2", target_bir_lowering=False, num_devices=1)
    arrays, args = {}, []
    for name in _INS:
        a = np.ascontiguousarray(inputs[name])
        arrays[f"in_{name}"] = a
        args.append(nc.dram_tensor(f"in_{name}", a.shape, mybir.dt.from_np(a.dtype), kind="ExternalInput").ap())
    shape = inputs["x"].shape
    args.append(nc.dram_tensor("out", shape, F32, kind="ExternalOutput").ap())
    build(nc, *args)
    return run_bass_kernel_spmd(nc, [arrays], core_ids=[0]).results[0]["out"]
```

```python
from contextlib import ExitStack

import concourse.bass as bass
from concourse import mybir

F32 = mybir.dt.float32
F32R = mybir.dt.float32r
I32 = mybir.dt.int32
ALU = mybir.AluOpType
ACT = mybir.ActivationFunctionType

P = 128
HI, LO = 0, 1
PASSES = ((HI, HI), (HI, LO), (LO, HI))
EPS = 1e-6


def wait(eng, sem, count):
    if not isinstance(count, int) or count > 0:
        eng.wait_ge(sem, count)


def build(nc, x, c, ada_w, ada_b, pre_norm_w, w_in, gla_gate_w2, gla_gate_b, gla_norm_w, conv_w, conv_b,
          dt_bias, a_log, d_skip, ssd_norm_w, w_out, post_norm_w, out):
    _, T, D = x.shape
    KT = D // P
    RANK, KEY = gla_gate_w2.shape[1:]
    DK = P
    GH = KEY // DK
    DV = gla_norm_w.shape[1]
    VAL = GH * DV
    SH = dt_bias.shape[1]
    SP_ = ssd_norm_w.shape[1] // SH
    INNER = SH * SP_
    TAPS, CONV = conv_w.shape[1:]
    NS = P
    G = (CONV - INNER) // (2 * NS)
    HG = SH // G
    GW = INNER // G
    XT = GW // P
    FT = (VAL + INNER) // P
    CH = 64
    assert DV == 2 * P and GW == 512 and SH == RANK == 16
    CQ, CK, CV = 0, KEY, 2 * KEY
    CG = CV + VAL
    CR = CG + VAL
    CZ = CR + RANK
    CX = CZ + INNER
    CD = CX + CONV

    B1 = 512
    NB = T // B1
    TB = B1 // P
    B2 = 256
    NB2 = T // B2
    TB2 = B2 // P

    w_rows = w_in[0].rearrange("(k p) n -> p k n", p=P)

    h_d = nc.dram_tensor("h", (NB, P, KT, B1), F32, kind="Internal").ap()
    ac_d = nc.dram_tensor("step_sums", (SH, T), F32, kind="Internal").ap()
    gate_d = nc.dram_tensor("gate_row", (1, D), F32, kind="Internal").ap()
    y_d = nc.dram_tensor("mixed_in", (NB2, P, FT, B2), F32, kind="Internal").ap()

    with ExitStack() as whole:
        ps = whole.enter_context(nc.psum_tensor("ps", [P, 8, 512], F32))
        ident = whole.enter_context(nc.sbuf_tensor("ident", [P, P], F32))
        with ExitStack() as parts:
            tok = parts.enter_context(nc.sbuf_tensor("tok", [P, T // P, 4, SH], F32))
            conv_col = parts.enter_context(nc.sbuf_tensor("conv_col", [P, TAPS, CONV // P], F32))
            convb_col = parts.enter_context(nc.sbuf_tensor("convb_col", [P, CONV // P], F32))
            d_row = parts.enter_context(nc.sbuf_tensor("d_row", [P, SH], F32))
            ssd_norm_col = parts.enter_context(nc.sbuf_tensor("ssd_norm_col", [P, G * XT], F32))
            with (nc.sbuf_tensor("causal", [P, P], F32) as causal,
                  nc.sbuf_tensor("keep_row", [P, B1], F32) as keep_row,
                  nc.sbuf_tensor("code", [RANK, T], F32) as code):
                prologue(nc, x, c, ada_w, ada_b, pre_norm_w, w_rows, dt_bias, a_log, post_norm_w, ps, ident, causal,
                         gate_d, keep_row, tok, code, h_d, ac_d, D, KT, SH, RANK, CR, CD, B1, NB, TB)
                gla(nc, w_rows, gla_gate_w2, gla_gate_b, gla_norm_w, ps, ident, causal, keep_row, code, h_d, y_d,
                    conv_w, conv_b, d_skip, ssd_norm_w, conv_col, convb_col, d_row, ssd_norm_col, KT, GH, DK, DV,
                    RANK, TAPS, CQ, CK, CV, CG, CH, B1, NB, TB, B2)
            ssd(nc, w_rows, conv_col, convb_col, d_row, ssd_norm_col, ps, ident, tok, h_d, ac_d, y_d, T, KT, G, HG, GW,
                XT, NS, SP_, INNER, VAL, TAPS, CZ, CX, B2, TB2)
        project_out(nc, x, w_out, out, ps, gate_d, y_d, D, FT, NB2, B2, TB2)


def prologue(nc, x, c, ada_w, ada_b, pre_norm_w, w_rows, dt_bias, a_log, post_norm_w, ps, ident, causal, gate_d,
             keep_row, tok, code, h_d, ac_d, D, KT, SH, RANK, CR, CD, B1, NB, TB):
    R0 = 32
    RS = slice(R0, R0 + SH)
    TURN, PACK, ROWS, GATE = 0, 3, 4, 5
    CODES = (2, 7)
    with ExitStack() as ctx:
        def sb(name, shape, dt=F32):
            return ctx.enter_context(nc.sbuf_tensor(name, shape, dt))

        def sem(name):
            return ctx.enter_context(nc.semaphore(name))

        ada = sb("ada", [P, KT, 2 * D])
        c_col = sb("c_col", [P, KT])
        c_act = sb("c_act", [P, KT])
        c_wide = sb("c_wide", [P, KT, P])
        one = sb("one", [1, 1])
        mod_row = ada[0:1, KT - 1, :]
        ada_col = sb("ada_col", [P, 2 * KT])
        pre_col = sb("pre_col", [P, KT])
        mod = sb("mod", [P, 2 * KT])
        gain = sb("gain", [P, KT])
        ada_row = ada[:, 0, D:2 * D]
        post_row = ada[:, 1, D:2 * D]
        gate_row = sb("a_gate_row", [P, D])
        x_sb = sb("x_sb", [P, NB, TB, D])
        squares = sb("squares", [P, D])
        ms = sb("ms", [P, NB, TB])
        mse = sb("mse", [P, NB, TB])
        rstd = sb("rstd", [P, NB, TB])
        neg_half = sb("neg_half", [P, TB])
        hf = sb("hf", [P, 2, KT, B1])
        wg = sb("wg", [P, KT, R0 + SH])
        dtb = sb("dtb", [P, 1])
        alog = sb("alog", [P, 1])
        aexp = sb("aexp", [P, 1])
        dtx = sb("dtx", [P, B1])
        dsoft = sb("dsoft", [P, B1])
        dta = sb("dta", [P, B1])
        dlast = sb("dlast", [P, B1])
        pack = sb("pack", [P, 4, B1])

        passed = sem("a_passed")
        consts_ready = sem("a_consts"); loads = sem("a_loads"); c_loaded = sem("a_c_loaded"); cols_loaded = sem("a_cols_loaded"); wg_loaded = sem("a_wg_loaded")
        ada_loaded = [sem(f"a_ada_loaded{i}") for i in range(KT)]
        gate_loaded = sem("a_gate_loaded"); gate_stored = sem("a_gate_stored")
        c_ready = sem("a_c_ready"); wide_ready = sem("a_wide_ready")
        mod_done = sem("a_mod_done"); row_ready = sem("a_row_ready"); cols_done = sem("a_cols_done")
        gate_done = sem("a_gate_done"); mod_ready = sem("a_mod_ready")
        gain_ready = sem("a_gain_ready"); gate_ready = sem("a_gate_ready")
        a_ready = sem("a_a_ready")
        x_loaded = [sem(f"a_x_loaded{i}") for i in range(NB)]
        ms_ready = sem("a_ms_ready"); mse_ready = sem("a_mse_ready"); rstd_ready = sem("a_rstd_ready")
        xn_ready = sem("a_xn_ready"); turned = sem("a_turned")
        even_ready = sem("a_even_ready"); odd_ready = sem("a_odd_ready")
        h_stored = [sem(f"a_h_stored{i}") for i in range(2)]
        codes_done = sem("a_codes_done"); dtx_ready = sem("a_dtx_ready")
        dsoft_step = sem("a_dsoft_step"); dt_ready = sem("a_dt_ready"); dta_ready = sem("a_dta_ready")
        acum_ready = sem("a_acum_ready"); dlast_ready = sem("a_dlast_ready"); pack_ready = sem("a_pack_ready")
        acum_stored = sem("a_acum_stored"); packed = sem("a_packed"); tok_ready = sem("a_tok_ready")

        def wait_h(eng, b, k):
            wait(eng, odd_ready if k % 2 else even_ready, b * (KT // 2) + k // 2 + 1)

        def blocks(step):
            for m in range(NB):
                step(m, m % 2)

        with nc.Block() as block:
            @block.sync
            def _(sp):
                def load_x(b):
                    sp.dma_start(x_sb[:, b], x[0, b * B1:(b + 1) * B1, :].rearrange("(t p) n -> p t n", p=P)
                                 ).then_inc(x_loaded[b], 16)

                sp.dma_start(c_col[:, :], c.rearrange("a (k p) -> p (a k)", p=P), allow_slow_non_contiguous=True).then_inc(c_loaded, 16)
                for k in range(KT):
                    sp.dma_start(ada[:, k, :], ada_w[0, k * P:(k + 1) * P, 0:2 * D]).then_inc(ada_loaded[k], 16)
                    if k == 1:
                        load_x(0)
                load_x(1)
                sp.wait_ge(mod_done, 1)
                for b in range(2, NB):
                    load_x(b)

                def step(m, par):
                    if m == NB - 2:
                        sp.wait_ge(cols_done, 1)
                        sp.dma_start(ada[:, :, 0:D], ada_w[0, :, 2 * D:3 * D].rearrange("(k p) n -> p k n", p=P)
                                     ).then_inc(gate_loaded, 16)
                        sp.dma_start(ada_row, ada_b[0, 2 * D:3 * D].partition_broadcast(P)).then_inc(gate_loaded, 16)
                        sp.dma_start(post_row, post_norm_w[0].partition_broadcast(P)).then_inc(gate_loaded, 16)
                    for half in range(2):
                        ks = slice(half * KT // 2, (half + 1) * KT // 2)
                        for k in (ks.stop - 2, ks.stop - 1):
                            wait_h(sp, m, k)
                        sp.dma_start(h_d[bass.ds(m, 1), :, ks].rearrange("a p k n -> (a p) k n"), hf[:, par, ks]
                                     ).then_inc(h_stored[par], 16)
                        if half == 1 and m > 0:
                            store_sums(m - 1)

                def store_sums(b):
                    sp.wait_ge(acum_ready, b + 1)
                    sp.dma_start(ac_d[:, bass.ds(b * B1, B1)], pack[RS, 1, :]).then_inc(acum_stored, 16)

                blocks(step)
                store_sums(NB - 1)
                sp.wait_ge(gate_ready, 2)
                sp.dma_start(gate_d, gate_row[0:1, :]).then_inc(gate_stored, 16)
                sp.wait_ge(gate_stored, 16)
                for s in h_stored:
                    sp.wait_ge(s, 16 * NB)
                sp.wait_ge(acum_stored, 16 * NB)

            @block.gpsimd
            def _(pool):
                pool.dma_start(ada_col[:, :], ada_b[0, 0:2 * D].rearrange("(k p) -> p k", p=P), allow_slow_non_contiguous=True).then_inc(cols_loaded, 16)
                pool.dma_start(pre_col[:, :], pre_norm_w[0].rearrange("(k p) -> p k", p=P), allow_slow_non_contiguous=True).then_inc(cols_loaded, 16)
                pool.memset(ident[:, :], 0.0).then_inc(consts_ready, 1)
                pool.memset(causal[:, :], 1.0).then_inc(consts_ready, 1)
                pool.memset(keep_row[:, :], 1.0).then_inc(consts_ready, 1)
                pool.memset(neg_half[:, :], -0.5).then_inc(consts_ready, 1)
                pool.memset(wg[:, :, :], 0.0).then_inc(consts_ready, 1)
                pool.memset(one[:, :], 1.0).then_inc(consts_ready, 1)
                pool.wait_ge(consts_ready, 6)
                pool.affine_select(out=ident[:, :], in_=ident[:, :], compare_op=ALU.not_equal, fill=1.0,
                                   base=0, pattern=[[-1, P]], channel_multiplier=1).then_inc(consts_ready, 1)
                pool.affine_select(out=causal[:, :], in_=causal[:, :], compare_op=ALU.is_ge, fill=0.0,
                                   base=0, pattern=[[1, P]], channel_multiplier=-1).then_inc(consts_ready, 1)
                pool.memset(keep_row[:, :].rearrange("p (t n) -> p t n", n=P)[:, :, 0:1], 0.0).then_inc(consts_ready, 1)
                pool.dma_start(wg[:, :, 0:RANK], w_rows[:, :, CR:CR + RANK]).then_inc(wg_loaded, 16)
                pool.dma_start(wg[:, :, R0:R0 + SH], w_rows[:, :, CD:CD + SH]).then_inc(wg_loaded, 16)
                pool.dma_start(dtb[RS, :], dt_bias.rearrange("a h -> h a"), allow_slow_non_contiguous=True).then_inc(loads, 16)
                pool.dma_start(alog[RS, :], a_log.rearrange("a h -> h a"), allow_slow_non_contiguous=True).then_inc(loads, 16)

                def rstds(b):
                    pool.wait_ge(ms_ready, b * TB + TB)
                    pool.tensor_scalar(mse[:, b, :], ms[:, b, :], EPS, None, ALU.add).then_inc(mse_ready, 1)
                    pool.wait_ge(mse_ready, b + 1)
                    pool.tensor_tensor(rstd[:, b, :], mse[:, b, :], neg_half[:, :], ALU.pow).then_inc(rstd_ready, 1)

                for b in range(NB):
                    rstds(b)

            @block.scalar
            def _(act):
                def square(b, t):
                    if t == 0:
                        act.wait_ge(x_loaded[b], 16)
                    wait(act, ms_ready, b * TB + t)
                    act.activation(squares[:, :], x_sb[:, b, t, :], ACT.Square, scale=D ** -0.5,
                                   accum_out=ms[:, b, t:t + 1]).then_inc(ms_ready, 1)

                def soft_sizes(b):
                    act.wait_ge(dtx_ready, b + 1)
                    wait(act, dt_ready, b)
                    act.activation(dsoft[RS, :], dtx[RS, :], ACT.Abs).then_inc(dsoft_step, 1)
                    act.wait_ge(dsoft_step, b * 3 + 1)
                    act.activation(dsoft[RS, :], dsoft[RS, :], ACT.Exp, scale=-1.0).then_inc(dsoft_step, 1)
                    act.wait_ge(dsoft_step, b * 3 + 2)
                    act.activation(dsoft[RS, :], dsoft[RS, :], ACT.Ln, bias=1.0).then_inc(dsoft_step, 1)

                def size_exps(b):
                    act.wait_ge(acum_ready, b + 1)
                    wait(act, packed, b)
                    act.activation(pack[RS, 2, :], pack[RS, 1, :], ACT.Exp).then_inc(pack_ready, 1)
                    act.wait_ge(dlast_ready, b + 1)
                    act.activation(pack[RS, 3, :], dlast[RS, :], ACT.Exp).then_inc(pack_ready, 1)

                def step(m, par):
                    wait(act, h_stored[par], m // 2 * 32)
                    for k in range(KT):
                        if k % 2 == 0:
                            act.wait_ge(turned, m * KT + k + 1)
                            wait_h(act, m, k - 2) if k >= 2 else wait(act, even_ready, m * (KT // 2))
                            act.activation(hf[:, par, k, :], ps[:, TURN + k % 2, :], ACT.Identity,
                                           scale=gain[:, k:k + 1], bias=mod[:, k:k + 1]).then_inc(even_ready, 1)
                        if k % 2 == 1 and m + 2 < NB:
                            square(m + 2, k // 2)
                        if k == 2 and m > 0:
                            soft_sizes(m - 1)
                        if k == 6 and m > 0:
                            size_exps(m - 1)
                    if m == 0:
                        act.wait_ge(loads, 32)
                        act.activation(aexp[RS, :], alog[RS, :], ACT.Exp).then_inc(a_ready, 1)
                    act.wait_ge(codes_done, m + 1)
                    act.activation(code[:, bass.ds(m * B1, B1)], ps[0:RANK, CODES[par], :], ACT.Copy)
                    wait(act, dt_ready, m)
                    act.activation(dtx[RS, :], ps[RS, CODES[par], :], ACT.Identity, bias=dtb[RS, :]).then_inc(dtx_ready, 1)

                act.wait_ge(c_loaded, 16)
                act.activation(c_act[:, :], c_col[:, :], ACT.Silu).then_inc(c_ready, 1)
                act.preload_act_table_set("natural_log_exp_and_others")
                for t in range(TB):
                    square(0, t)
                act.wait_ge(mod_done, 1)
                act.activation(mod_row[:, 0:D], ps[0:1, ROWS:ROWS + 2, :].rearrange("p a n -> p (a n)"),
                               ACT.Copy).then_inc(row_ready, 1)
                for t in range(TB):
                    square(1, t)
                act.wait_ge(gain_ready, 1)
                blocks(step)
                soft_sizes(NB - 1)
                size_exps(NB - 1)

            @block.vector
            def _(dve):
                def normed(b, tiles):
                    dve.wait_ge(rstd_ready, b + 1)
                    for t in tiles:
                        dve.tensor_scalar(x_sb[:, b, t, :], x_sb[:, b, t, :], rstd[:, b, t:t + 1], None,
                                          ALU.mult).then_inc(xn_ready, 1)

                def sizes(b):
                    if b == 0:
                        dve.wait_ge(a_ready, 1)
                        dve.wait_ge(loads, 32)
                        dve.tensor_scalar(alog[RS, :], aexp[RS, :], -1.0, None, ALU.mult).then_inc(a_ready, 1)
                        dve.wait_ge(a_ready, 2)
                    dve.wait_ge(dsoft_step, b * 3 + 3)
                    wait(dve, packed, b)
                    dve.scalar_tensor_tensor(out=pack[RS, 0, :], in0=dtx[RS, :], scalar=0.0, in1=dsoft[RS, :],
                                             op0=ALU.max, op1=ALU.add).then_inc(dt_ready, 1)
                    dve.wait_ge(dt_ready, b + 1)
                    dve.tensor_scalar(dta[RS, :], pack[RS, 0, :], alog[RS, :], None, ALU.mult).then_inc(dta_ready, 1)
                    dve.wait_ge(dta_ready, b + 1)
                    wait(dve, acum_stored, b * 16)
                    dve.tensor_tensor_scan(pack[RS, 1, :], keep_row[RS, :], dta[RS, :], 0.0, ALU.mult,
                                           ALU.add).then_inc(acum_ready, 1)
                    dve.wait_ge(acum_ready, b + 1)
                    wait(dve, pack_ready, b * 2)
                    tiles = pack[RS, 1, :].rearrange("h (t n) -> h t n", n=P)
                    dve.tensor_tensor(dlast[RS, :].rearrange("h (t n) -> h t n", n=P),
                                      tiles[:, :, P - 1:P].broadcast_to([SH, TB, P]), tiles,
                                      ALU.subtract).then_inc(dlast_ready, 1)

                def keep_sizes(b):
                    dve.wait_ge(packed, b + 1)
                    dve.tensor_copy(tok[:, bass.ds(b * TB, TB), :, :].rearrange("p t q h -> p (t q h)"),
                                    ps[:, PACK, 0:TB * 4 * SH]).then_inc(tok_ready, 1)

                def step(m, par):
                    wait(dve, h_stored[par], m // 2 * 32)
                    for k in range(1, KT, 2):
                        dve.wait_ge(turned, m * KT + k + 1)
                        wait_h(dve, m, k - 2) if k >= 2 else wait(dve, odd_ready, m * (KT // 2))
                        dve.tensor_scalar(hf[:, par, k, :], ps[:, TURN + k % 2, :], gain[:, k:k + 1],
                                          mod[:, k:k + 1], ALU.mult, ALU.add).then_inc(odd_ready, 1)
                        if k == 1 and m < NB - 1:
                            normed(m + 1, range(TB // 2))
                        if k == 1 and m > 1:
                            keep_sizes(m - 2)
                        if k == 3 and m < NB - 1:
                            normed(m + 1, range(TB // 2, TB))
                        if k == 5 and m > 0:
                            sizes(m - 1)

                dve.wait_ge(c_ready, 1)
                dve.tensor_copy(c_wide[:, :, :], c_act[:, :].unsqueeze(2).broadcast_to([P, KT, P])).then_inc(wide_ready, 1)
                normed(0, range(TB))
                dve.wait_ge(mod_done, 1)
                dve.tensor_copy(mod_row[:, D:2 * D], ps[0:1, ROWS + 2:ROWS + 4, :].rearrange("p a n -> p (a n)")
                                ).then_inc(row_ready, 1)
                dve.wait_ge(cols_done, 1)
                dve.wait_ge(cols_loaded, 32)
                dve.tensor_tensor(mod[:, :], ps[:, PACK, 0:2 * KT], ada_col[:, :], ALU.add).then_inc(mod_ready, 1)
                dve.wait_ge(mod_ready, 1)
                dve.scalar_tensor_tensor(out=gain[:, :], in0=mod[:, KT:2 * KT], scalar=1.0, in1=pre_col[:, :],
                                         op0=ALU.add, op1=ALU.mult).then_inc(gain_ready, 1)
                dve.wait_ge(gain_ready, 1)
                dve.wait_ge(consts_ready, 9)
                blocks(step)
                keep_sizes(NB - 2)
                sizes(NB - 1)
                dve.wait_ge(gate_done, 1)
                dve.wait_ge(gate_loaded, 48)
                dve.tensor_tensor(gate_row[:, :], ps[:, GATE:GATE + 2, :].rearrange("p a n -> p (a n)"), ada_row,
                                  ALU.add).then_inc(gate_ready, 1)
                dve.wait_ge(gate_ready, 1)
                dve.tensor_tensor(gate_row[:, :], gate_row[:, :], post_row, ALU.mult).then_inc(gate_ready, 1)
                keep_sizes(NB - 1)

            @block.tensor
            def _(pe):
                pe.wait_ge(c_ready, 1)
                for k in range(KT):
                    pe.wait_ge(ada_loaded[k], 16)
                    for j in range(2 * D // 512):
                        mm = pe.matmul(ps[0:1, ROWS + j, :], c_act[:, k:k + 1], ada[:, k, j * 512:(j + 1) * 512],
                                       start=(k == 0), stop=(k == KT - 1))
                mm.then_inc(mod_done, 1)
                pe.wait_ge(consts_ready, 9)
                pe.wait_ge(row_ready, 2)
                for f in range(2 * KT):
                    mm = pe.matmul(ps[:, PACK, f:f + 1], mod_row[:, f * P:(f + 1) * P], one[:, :], start=True, stop=True)
                mm.then_inc(cols_done, 1)
                pe.wait_ge(wg_loaded, 32)
                pe.wait_ge(mod_ready, 1)

                def codes(m, par, k):
                    wait_h(pe, m, k)
                    mm = pe.matmul(ps[0:R0 + SH, CODES[par], :], wg[:, k, :], hf[:, par, k, :],
                                   start=(k == 0), stop=(k == KT - 1))
                    if k == KT - 1:
                        mm.then_inc(codes_done, 1)

                def turn_sizes(b):
                    pe.wait_ge(pack_ready, b * 2 + 2)
                    wait(pe, tok_ready, b)
                    pe.sem_inc(passed, 1)
                    for t in range(TB):
                        for q in range(4):
                            o = (t * 4 + q) * SH
                            mm = pe.transpose(ps[:, PACK, o:o + SH], pack[RS, q, t * P:(t + 1) * P], ident[RS, RS])
                    mm.then_inc(packed, 1)

                def step(m, par):
                    pe.wait_ge(xn_ready, m * TB + TB)
                    wait(pe, dtx_ready, m - 1)
                    for k in range(KT):
                        if k >= 2:
                            wait_h(pe, m, k - 2)
                        elif m > 0:
                            wait_h(pe, m - 1, KT - 2 + k)
                        for t in range(TB):
                            mm = pe.transpose(ps[:, TURN + k % 2, t * P:(t + 1) * P], x_sb[:, m, t, k * P:(k + 1) * P],
                                              ident[:, :])
                        mm.then_inc(turned, 1)
                        if k > 0:
                            codes(m, par, k - 1)
                        if k == 7 and m > 0:
                            turn_sizes(m - 1)
                    codes(m, par, KT - 1)

                blocks(step)
                pe.wait_ge(wide_ready, 1)
                pe.wait_ge(gate_loaded, 48)
                for j in range(2):
                    for k in range(KT):
                        mm = pe.matmul(ps[:, GATE + j, :], c_wide[:, k, :], ada[:, k, j * 512:(j + 1) * 512],
                                       start=(k == 0), stop=(k == KT - 1))
                mm.then_inc(gate_done, 1)
                turn_sizes(NB - 1)


def gla(nc, w_rows, gla_gate_w2, gla_gate_b, gla_norm_w, ps, ident, causal, keep_row, code, h_d, y_d, conv_w, conv_b,
        d_skip, ssd_norm_w, conv_col, convb_col, d_row, ssd_norm_col, KT, GH, DK, DV, RANK, TAPS, CQ, CK, CV, CG,
        CH, B1, NB, TB, B2):
    U = 6
    UQ, UK, UG, UV = 0, 1, 2, 4
    TAU = 16.0
    PROJ, KTURN, AT, O, KV, OT, GATE = 0, 2, 3, 4, 5, 6, 7
    QK = 2
    QS = KT // QK
    with ExitStack() as ctx:
        def sb(name, shape, dt=F32):
            return ctx.enter_context(nc.sbuf_tensor(name, shape, dt))

        def sem(name):
            return ctx.enter_context(nc.semaphore(name))

        hl = sb("b_hl", [P, 2, KT, 2, B1], F32R)
        w = sb("b_w", [P, UV, KT, 2, P], F32R)
        w_v = sb("b_w_v", [P, KT, 2, DV], F32R)
        w_raw = sb("b_w_raw", [P, 2, KT, P])
        h_raw = sb("b_h_raw", [P, 2, QK, B1])
        w2 = sb("b_w2", [RANK, GH * DK])
        gb = sb("b_gb", [P, GH])
        w2_h = sb("b_w2_h", [RANK, DK])
        gb_h = sb("b_gb_h", [P, 1])
        xg = sb("b_xg", [P, B1])
        soft = sb("b_soft", [P, B1])
        sums = sb("b_sums", [P, B1])
        qk = sb("b_qk", [P, 2, B1])
        gz = sb("b_gz", [P, 2, 2, B1])
        v = sb("b_v", [P, 2, TB, DV])
        e_all = sb("b_e_all", [P, B1])
        e_mid = sb("b_e_mid", [P, B1])
        e_end = sb("b_e_end", [P, B1])
        e_qmid = sb("b_e_qmid", [P, B1])
        q_all = sb("b_q_all", [P, B1])
        q_mid = sb("b_q_mid", [P, B1])
        k_mid = sb("b_k_mid", [P, B1])
        k_end = sb("b_k_end", [P, B1])
        dec = sb("b_dec", [P, TB])
        k_tok = sb("b_k_tok", [P, DK])
        att = sb("b_att", [P, P])
        state = sb("b_state", [P, DV])
        squares = sb("b_squares", [P, DV])
        ms = sb("b_ms", [P, 1])
        mse = sb("b_mse", [P, 1])
        rstd = sb("b_rstd", [P, 1])
        neg_half = sb("b_neg_half", [P, 1])
        o_n = sb("b_o_n", [P, DV])
        norm_col = sb("b_norm_col", [P, 2])
        y = sb("b_y", [P, 2, B1])

        h_loaded = [sem(f"b_h_loaded{i}") for i in range(2)]
        h_hi = sem("b_h_hi"); h_ready = sem("b_h_ready")
        small_loaded = sem("b_small_loaded"); w2_ready = sem("b_w2_ready"); gates_done = sem("b_gates_done")
        xg_ready = sem("b_xg_ready"); soft_step = sem("b_soft_step"); loga_ready = sem("b_loga_ready")
        sums_ready = sem("b_sums_ready")
        raw_loaded = [sem(f"b_raw_loaded{i}") for i in range(2)]
        passed = sem("b_passed")
        cols_loaded = sem("b_cols_loaded"); consts_ready = sem("b_consts")
        w_hi = sem("b_w_hi"); w_ready = sem("b_w_ready"); unit_done = sem("b_unit_done"); unit_out = sem("b_unit_out")
        gsilu = sem("b_gsilu"); qmid_ready = sem("b_qmid_ready"); d_ready = sem("b_d_ready"); exps_ready = sem("b_exps_ready"); prod_ready = sem("b_prod_ready")
        kt_done = sem("b_kt_done"); kt_ready = sem("b_kt_ready"); att_done = sem("b_att_done"); att_ready = sem("b_att_ready")
        o_done = sem("b_o_done"); kv_done = sem("b_kv_done"); state_ready = sem("b_state_ready")
        ms_ready = sem("b_ms_ready"); mse_ready = sem("b_mse_ready"); rstd_ready = sem("b_rstd_ready")
        on_ready = sem("b_on_ready"); ot_done = sem("b_ot_done"); y_ready = sem("b_y_ready"); y_stored = sem("b_y_stored")

        STEPS = GH * NB

        H_SLOTS = (1, 4, 7, 10)
        W_SLOTS = tuple(2 * u + 3 for u in range(UV))
        V_SLOTS = (1, 3)
        AHEAD = 3

        def part(u, p):
            return w[:, u, :, p, :] if u < UV else w_v[:, :, p, (u - UV) * P:(u - UV + 1) * P]

        def column(h, u):
            return (CQ + h * DK, CK + h * DK, CG + h * DV, CG + h * DV + P, CV + h * DV, CV + h * DV + P)[u]

        with nc.Block() as block:
            @block.sync
            def _(sp):
                def load_w(h, u):
                    wait(sp, w_ready, h * U + u - 1)
                    sp.dma_start(w_raw[:, u % 2], w_rows[:, :, bass.ds(column(h, u), P)]).then_inc(raw_loaded[u % 2], 16)

                def load_h(n, s, q):
                    wait(sp, h_ready, n * QS + q - 1)
                    sp.dma_start(h_raw[:, q % 2], h_d[s, :, q * QK:(q + 1) * QK, :]).then_inc(h_loaded[q % 2], 16)

                def store_y(n, h, s):
                    sp.wait_ge(y_ready, n * TB + TB)
                    for b in range(B1 // B2):
                        sp.dma_start(y_d[s * (B1 // B2) + b, :, bass.ds(h * 2, 2), :],
                                     y[:, :, b * B2:(b + 1) * B2]).then_inc(y_stored, 16)

                for u in range(U):
                    load_w(0, u)
                    if u < QS:
                        load_h(0, 0, u)

                def head(h, last):
                    for s in range(NB):
                        n = h * NB + s
                        if s < NB - 1 or not last:
                            for q in range(QS):
                                load_h(n + 1, (s + 1) % NB, q)
                                if s == NB - 1:
                                    for u in ((0, 1), (), (2,), (3, 4, 5))[q]:
                                        load_w(h + 1, u)
                        if s > 0:
                            store_y(n - 1, h, s - 1)
                        elif not isinstance(h, int) or h > 0:
                            store_y(n - 1, h - 1, NB - 1)

                head(0, False)
                with sp.Fori(1, GH - 1) as h:
                    head(h, False)
                head(GH - 1, True)
                store_y(STEPS - 1, GH - 1, NB - 1)
                sp.wait_ge(y_stored, 32 * STEPS)

            @block.gpsimd
            def _(pool):
                pool.memset(att[:, :], 0.0).then_inc(consts_ready, 1)
                pool.memset(neg_half[:, :], -0.5).then_inc(consts_ready, 1)
                pool.wait_ge(consts_ready, 2)
                pool.dma_start(w2[:, :], gla_gate_w2[0]).then_inc(small_loaded, 16)
                pool.dma_start(gb[:, :], gla_gate_b[0].rearrange("(h p) -> p h", p=P), allow_slow_non_contiguous=True).then_inc(small_loaded, 16)
                pool.dma_start(norm_col[:, :], gla_norm_w[0].rearrange("(k p) -> p k", p=P), allow_slow_non_contiguous=True).then_inc(small_loaded, 16)

                def rstd_of(r, t):
                    m = r * TB + t
                    pool.wait_ge(ms_ready, m + 1)
                    pool.sem_inc(passed, 1)
                    pool.tensor_scalar(mse[:, :], ms[:, :], EPS, None, ALU.add).then_inc(mse_ready, 1)
                    pool.wait_ge(mse_ready, m + 1)
                    wait(pool, on_ready, m)
                    pool.tensor_tensor(rstd[:, :], mse[:, :], neg_half[:, :], ALU.pow).then_inc(rstd_ready, 1)

                for t in range(TAPS):
                    pool.dma_start(conv_col[:, t, :], conv_w[0, t].rearrange("(k p) -> p k", p=P), allow_slow_non_contiguous=True).then_inc(cols_loaded, 16)
                pool.dma_start(convb_col[:, :], conv_b[0].rearrange("(k p) -> p k", p=P), allow_slow_non_contiguous=True).then_inc(cols_loaded, 16)
                pool.dma_start(d_row[:, :], d_skip[0].partition_broadcast(P)).then_inc(cols_loaded, 16)
                pool.dma_start(ssd_norm_col[:, :], ssd_norm_w[0].rearrange("(k p) -> p k", p=P), allow_slow_non_contiguous=True).then_inc(cols_loaded, 16)

                for t in range(TB):
                    rstd_of(0, t)
                with pool.Fori(1, STEPS) as r:
                    for t in range(TB):
                        rstd_of(r, t)
                pool.wait_ge(cols_loaded, 16 * (TAPS + 3))

            @block.scalar
            def _(act):
                def w_high(h, u):
                    act.wait_ge(raw_loaded[u % 2], (h * (U // 2) + u // 2 + 1) * 16)
                    wait(act, unit_done, (h * NB - 1) * U + (u + 1 if u < UV else U))
                    act.activation(part(u, HI), w_raw[:, u % 2], ACT.Copy).then_inc(w_hi, 1)

                def h_high(n, q, par):
                    act.wait_ge(h_loaded[q % 2], (n * (QS // 2) + q // 2 + 1) * 16)
                    wait(act, unit_done, (n - 1) * U)
                    act.activation(hl[:, par, q * QK:(q + 1) * QK, HI, :], h_raw[:, q % 2], ACT.Copy).then_inc(h_hi, 1)

                def soft_gate(n):
                    act.wait_ge(gates_done, n + 1)
                    wait(act, loga_ready, n)
                    act.activation(xg[:, :], ps[:, GATE, :], ACT.Identity, bias=gb_h[:, :]).then_inc(xg_ready, 1)
                    act.wait_ge(xg_ready, n + 1)
                    act.activation(soft[:, :], xg[:, :], ACT.Abs).then_inc(soft_step, 1)
                    act.wait_ge(soft_step, n * 3 + 1)
                    act.activation(soft[:, :], soft[:, :], ACT.Exp, scale=-1.0).then_inc(soft_step, 1)
                    act.wait_ge(soft_step, n * 3 + 2)
                    act.activation(soft[:, :], soft[:, :], ACT.Ln, bias=1.0).then_inc(soft_step, 1)

                def evacuate(n, u, par):
                    act.wait_ge(unit_done, n * U + u + 1)
                    if u in (UQ, UK):
                        wait(act, prod_ready, n)
                        dst = qk[:, u - UQ, :]
                    elif u in (UG, UG + 1):
                        wait(act, y_ready, (n - 1) * TB)
                        dst = gz[:, par, u - UG, :]
                    else:
                        wait(act, kv_done, (n - 1) * TB)
                        dst = v[:, par, (u - UV) * 2:(u - UV) * 2 + 2, :].rearrange("p t n -> p (t n)")
                    act.activation(dst, ps[:, PROJ + u % 2, :], ACT.Copy).then_inc(unit_out, 1)

                def exps(n):
                    act.wait_ge(d_ready, n + 1)
                    act.activation(e_all[:, :], sums[:, :], ACT.Exp, scale=1.0 / TAU)
                    act.activation(e_qmid[:, :], e_mid[:, :], ACT.Exp, scale=-1.0 / TAU).then_inc(qmid_ready, 1)
                    act.wait_ge(qmid_ready, n + 1)
                    act.activation(e_mid[:, :], e_mid[:, :], ACT.Exp, scale=1.0 / TAU)
                    act.activation(e_end[:, :], e_end[:, :], ACT.Exp, scale=1.0 / TAU).then_inc(exps_ready, 1)

                def silu_gate(n, par):
                    act.wait_ge(unit_out, n * U + UG + 2)
                    act.activation(gz[:, par], gz[:, par], ACT.Silu).then_inc(gsilu, 1)

                def kt_copy(r, t):
                    m = r * TB + t
                    act.wait_ge(kt_done, m + 1)
                    wait(act, kv_done, m)
                    act.activation(k_tok[:, :], ps[:, KTURN, 0:DK], ACT.Copy).then_inc(kt_ready, 1)

                def normed(r, t):
                    m = r * TB + t
                    act.wait_ge(o_done, m + 1)
                    wait(act, mse_ready, m)
                    wait(act, ms_ready, m)
                    act.activation(squares[:, :], ps[:, O, 0:DV], ACT.Square, scale=DV ** -0.5,
                                   accum_out=ms[:, :]).then_inc(ms_ready, 1)
                    act.wait_ge(rstd_ready, m + 1)
                    wait(act, ot_done, m)
                    act.activation(o_n[:, :], ps[:, O, 0:DV], ACT.Copy, scale=rstd[:, :]).then_inc(on_ready, 1)

                def step(n, h, s, first, last):
                    par = s % 2
                    for i in range(3 * TB):
                        if i % 2 == 1:
                            evacuate(n, i // 2, par)
                        if not first and i % 3 == 0:
                            kt_copy(n - 1, i // 3)
                        if i == (3 if first else 2):
                            soft_gate(n)
                        if not first and i % 3 == 1:
                            normed(n - 1, i // 3)
                        if i % 2 == 1 and first and i // 2 + AHEAD < U:
                            w_high(0, i // 2 + AHEAD)
                        if i in V_SLOTS and s == 0 and not first:
                            w_high(h, UV + V_SLOTS.index(i))
                        if i == 5:
                            exps(n)
                        if i == 7:
                            silu_gate(n, par)
                        if i in H_SLOTS and not last:
                            h_high(n + 1, H_SLOTS.index(i), 1 - par)
                        if i in W_SLOTS and s == NB - 1 and not last:
                            w_high(h + 1, W_SLOTS.index(i))

                for q in range(QS):
                    if q < AHEAD:
                        w_high(0, q)
                    h_high(0, q, 0)
                step(0, 0, 0, True, False)
                for s in range(1, NB):
                    step(s, 0, s, False, False)
                with act.Fori(1, GH - 1) as h:
                    for s in range(NB):
                        step(h * NB + s, h, s, False, False)
                for s in range(NB):
                    step(STEPS - NB + s, GH - 1, s, False, s == NB - 1)
                kt_copy(STEPS - 1, 0)
                for t in range(TB):
                    if t < TB - 1:
                        kt_copy(STEPS - 1, t + 1)
                    normed(STEPS - 1, t)

            @block.vector
            def _(dve):

                def w_low(h, u):
                    dve.wait_ge(w_hi, h * U + u + 1)
                    dve.tensor_tensor(part(u, LO), w_raw[:, u % 2], part(u, HI).bitcast(F32),
                                      ALU.subtract).then_inc(w_ready, 1)

                def h_low(n, q, par):
                    dve.wait_ge(h_hi, n * QS + q + 1)
                    ks = slice(q * QK, (q + 1) * QK)
                    dve.tensor_tensor(hl[:, par, ks, LO, :], h_raw[:, q % 2], hl[:, par, ks, HI, :].bitcast(F32),
                                      ALU.subtract).then_inc(h_ready, 1)

                def head_gate(h):
                    wait(dve, gates_done, h * NB)
                    wait(dve, xg_ready, h * NB)
                    dve.tensor_copy(w2_h[:, :], w2[:, bass.ds(h * DK, DK)]).then_inc(w2_ready, 1)
                    dve.tensor_copy(gb_h[:, :], gb[:, bass.ds(h, 1)]).then_inc(w2_ready, 1)

                def gate_sums(n):
                    dve.wait_ge(soft_step, n * 3 + 3)
                    dve.scalar_tensor_tensor(out=xg[:, :], in0=xg[:, :], scalar=0.0, in1=soft[:, :],
                                             op0=ALU.min, op1=ALU.subtract).then_inc(loga_ready, 1)
                    dve.wait_ge(loga_ready, n + 1)
                    wait(dve, exps_ready, n)
                    dve.tensor_tensor_scan(sums[:, :], keep_row[:, :], xg[:, :], 0.0, ALU.mult,
                                           ALU.add).then_inc(sums_ready, 1)

                def differences(n):
                    dve.wait_ge(sums_ready, n + 1)
                    wait(dve, prod_ready, n)
                    cb = sums[:, :].rearrange("p (t n) -> p t n", n=P)
                    dve.tensor_tensor(e_mid[:, :].rearrange("p (t n) -> p t n", n=P),
                                      cb[:, :, CH - 1:CH].broadcast_to([P, TB, P]), cb, ALU.subtract)
                    dve.tensor_tensor(e_end[:, :].rearrange("p (t n) -> p t n", n=P),
                                      cb[:, :, P - 1:P].broadcast_to([P, TB, P]), cb, ALU.subtract).then_inc(d_ready, 1)

                def products(n):
                    dve.wait_ge(unit_out, n * U + UK + 1)
                    dve.wait_ge(exps_ready, n + 1)
                    wait(dve, kv_done, n * TB)
                    wait(dve, state_ready, n * TB)
                    scale = DK ** -0.5
                    dve.scalar_tensor_tensor(out=q_all[:, :], in0=qk[:, 0, :], scalar=scale, in1=e_all[:, :],
                                             op0=ALU.mult, op1=ALU.mult)
                    dve.scalar_tensor_tensor(out=q_mid[:, :], in0=qk[:, 0, :], scalar=scale, in1=e_qmid[:, :],
                                             op0=ALU.mult, op1=ALU.mult)
                    dve.tensor_tensor(k_mid[:, :], qk[:, 1, :], e_mid[:, :], ALU.mult)
                    dve.tensor_tensor(k_end[:, :], qk[:, 1, :], e_end[:, :], ALU.mult)
                    dve.tensor_copy(dec[:, :], e_all[:, :].rearrange("p (t n) -> p t n", n=P)[:, :, P - 1]).then_inc(prod_ready, 1)

                def mask_att(r, t):
                    m = r * TB + t
                    dve.wait_ge(att_done, m + 1)
                    wait(dve, o_done, m)
                    dve.sem_inc(passed, 1)
                    dve.copy_predicated(att[:, :], causal[:, :].bitcast(I32), ps[:, AT, 0:P]).then_inc(att_ready, 1)

                def update_state(r, t, fresh):
                    m = r * TB + t
                    dve.wait_ge(kv_done, m + 1)
                    dve.wait_ge(prod_ready, r + 1)
                    if fresh:
                        dve.tensor_copy(state[:, :], ps[:, KV, 0:DV]).then_inc(state_ready, 1)
                    else:
                        dve.wait_ge(state_ready, m)
                        dve.scalar_tensor_tensor(out=state[:, :], in0=state[:, :], scalar=dec[:, t:t + 1],
                                                 in1=ps[:, KV, 0:DV], op0=ALU.mult, op1=ALU.add).then_inc(state_ready, 1)

                def gated(r, t, par):
                    m = r * TB + t
                    dve.wait_ge(ot_done, m + 1)
                    if t == 0:
                        dve.wait_ge(gsilu, r + 1)
                        wait(dve, y_stored, r * 32)
                    for f in range(2):
                        last = dve.scalar_tensor_tensor(
                            out=y[:, f, t * P:(t + 1) * P], in0=ps[:, OT, f * P:(f + 1) * P], scalar=norm_col[:, f:f + 1],
                            in1=gz[:, par, f, t * P:(t + 1) * P], op0=ALU.mult, op1=ALU.mult)
                    last.then_inc(y_ready, 1)

                def step(n, h, s, first, last):
                    fresh = (s - 1) % NB == 0
                    for i in range(3 * TB):
                        t = i // 3
                        if i == 3 * TB - 1:
                            products(n)
                        if i % 3 == 0 and not first:
                            mask_att(n - 1, t)
                        if i % 3 == 1 and not first:
                            update_state(n - 1, t, fresh and t == 0)
                        if i % 3 == 2 and not first:
                            gated(n - 1, t, (s - 1) % 2)
                        if i == 3:
                            gate_sums(n)
                            differences(n)
                        if i % 2 == 1 and first and i // 2 + AHEAD < U:
                            w_low(0, i // 2 + AHEAD)
                        if i in V_SLOTS and s == 0 and not first:
                            w_low(h, UV + V_SLOTS.index(i))
                        if i == 9 and s == NB - 1 and not last:
                            head_gate(h + 1)
                        if i in H_SLOTS and not last:
                            h_low(n + 1, H_SLOTS.index(i), (s + 1) % 2)
                        if i in W_SLOTS and s == NB - 1 and not last:
                            w_low(h + 1, W_SLOTS.index(i))

                for q in range(QS):
                    if q < AHEAD:
                        w_low(0, q)
                    h_low(0, q, 0)
                dve.wait_ge(consts_ready, 2)
                dve.wait_ge(small_loaded, 48)
                head_gate(0)
                step(0, 0, 0, True, False)
                for s in range(1, NB):
                    step(s, 0, s, False, False)
                with dve.Fori(1, GH - 1) as h:
                    for s in range(NB):
                        step(h * NB + s, h, s, False, False)
                for s in range(NB):
                    step(STEPS - NB + s, GH - 1, s, False, s == NB - 1)
                mask_att(STEPS - 1, 0)
                for t in range(TB):
                    if t < TB - 1:
                        mask_att(STEPS - 1, t + 1)
                    update_state(STEPS - 1, t, False)
                    if t > 0:
                        gated(STEPS - 1, t - 1, (NB - 1) % 2)
                gated(STEPS - 1, TB - 1, (NB - 1) % 2)

            @block.tensor
            def _(pe):
                def half_unit(n, h, u, half, par):
                    if half == 0:
                        pe.wait_ge(w_ready, h * U + (u + 1 if u < UV else U))
                        wait(pe, unit_out, n * U + u - 1)
                    if u < UV:
                        for k in range(half * KT // 2, (half + 1) * KT // 2):
                            if u == 0 and k % QK == 0:
                                pe.wait_ge(h_ready, n * QS + k // QK + 1)
                            for i, (a, b) in enumerate(PASSES):
                                mm = pe.matmul(ps[:, PROJ + u % 2, :], w[:, u, k, a, :], hl[:, par, k, b, :],
                                               start=(k == 0 and i == 0), stop=(k == KT - 1 and i == 2))
                    else:
                        t = (u - UV) * 2 + half
                        for k in range(KT):
                            for i, (a, b) in enumerate(PASSES):
                                mm = pe.matmul(ps[:, PROJ + u % 2, half * DV:(half + 1) * DV],
                                               hl[:, par, k, a, t * P:(t + 1) * P], w_v[:, k, b, :],
                                               start=(k == 0 and i == 0), stop=(k == KT - 1 and i == 2))
                    if half == 1:
                        mm.then_inc(unit_done, 1)

                def scores(r, t):
                    m = r * TB + t
                    if t == 0:
                        pe.wait_ge(prod_ready, r + 1)
                    wait(pe, kt_ready, m)
                    cols = slice(t * P, (t + 1) * P)
                    pe.transpose(ps[:, KTURN, 0:DK], k_end[:, cols], ident[:, :]).then_inc(kt_done, 1)
                    wait(pe, att_ready, m)
                    pe.matmul(ps[:, AT, 0:P], k_mid[:, cols], q_mid[:, cols], start=True, stop=True).then_inc(att_done, 1)

                def outputs(r, t, fresh, par):
                    m = r * TB + t
                    wait(pe, on_ready, m)
                    pe.wait_ge(att_ready, m + 1)
                    pe.wait_ge(kt_ready, m + 1)
                    if t == 0:
                        pe.wait_ge(unit_out, r * U + U)
                    mm = pe.matmul(ps[:, O, 0:DV], att[:, :], v[:, par, t, :], start=True, stop=fresh)
                    if not fresh:
                        pe.wait_ge(state_ready, m)
                        mm = pe.matmul(ps[:, O, 0:DV], q_all[:, t * P:(t + 1) * P], state[:, :], start=False, stop=True)
                    mm.then_inc(o_done, 1)
                    wait(pe, state_ready, m)
                    pe.matmul(ps[:, KV, 0:DV], k_tok[:, :], v[:, par, t, :], start=True, stop=True).then_inc(kv_done, 1)

                def turn(r, t):
                    m = r * TB + t
                    pe.wait_ge(on_ready, m + 1)
                    wait(pe, y_ready, m)
                    for f in range(2):
                        mm = pe.transpose(ps[:, OT, f * P:(f + 1) * P], o_n[:, f * P:(f + 1) * P], ident[:, :])
                    mm.then_inc(ot_done, 1)

                def gates(n, h, s):
                    pe.wait_ge(w2_ready, h * 2 + 2)
                    wait(pe, xg_ready, n)
                    pe.matmul(ps[:, GATE, :], w2_h[:, :], code[:, s * B1:(s + 1) * B1], start=True,
                              stop=True).then_inc(gates_done, 1)

                def step(n, h, s, first):
                    par = s % 2
                    fresh = (s - 1) % NB == 0
                    for i in range(3 * TB):
                        t = i // 3
                        half_unit(n, h, i // 2, i % 2, par)
                        if i == (3 if first else 0):
                            gates(n, h, s)
                        if not first:
                            if i % 3 == 0:
                                scores(n - 1, t)
                            if i % 3 == 1:
                                outputs(n - 1, t, fresh and t == 0, 1 - par)
                            if i % 3 == 2:
                                turn(n - 1, t)

                step(0, 0, 0, True)
                for s in range(1, NB):
                    step(s, 0, s, False)
                with pe.Fori(1, GH) as h:
                    for s in range(NB):
                        step(h * NB + s, h, s, False)
                scores(STEPS - 1, 0)
                for t in range(TB):
                    if t < TB - 1:
                        scores(STEPS - 1, t + 1)
                    outputs(STEPS - 1, t, False, (NB - 1) % 2)
                    if t > 0:
                        turn(STEPS - 1, t - 1)
                turn(STEPS - 1, TB - 1)


def ssd(nc, w_rows, conv_col, convb_col, d_row, norm_col, ps, ident, tok, h_d, ac_d, y_d, T, KT, G, HG, GW, XT, NS,
        SP_, INNER, VAL, TAPS, CZ, CX, B2, TB2):
    UB, UC, UX, UZ = 0, 1, 2, 2 + XT
    UCONV, U = UZ, UZ + XT
    UP = UZ + TB2
    S = T // B2
    HIST = TAPS - 1
    PROJ, X, BC, Y, YI, ST, YT = 0, 2, 3, 4, 5, 6, 7
    QS = 4
    QK = KT // QS
    with ExitStack() as ctx:
        def sb(name, shape, dt=F32):
            return ctx.enter_context(nc.sbuf_tensor(name, shape, dt))

        def sem(name):
            return ctx.enter_context(nc.semaphore(name))

        hl = sb("c_hl", [P, 2, KT, 2, B2], F32R)
        w = sb("c_w", [P, UZ, KT, 2, P], F32R)
        w_z = sb("c_w_z", [P, KT, 2, GW], F32R)
        w_raw = sb("c_w_raw", [P, 2, KT, P])
        h_raw = sb("c_h_raw", [P, 2, QK, B2])
        past = sb("c_past", [P, P])
        before = sb("c_before", [P, UCONV, HIST + B2])
        acc = sb("c_acc", [P, UCONV, B2])
        xbc = sb("c_xbc", [P, 2, UCONV, B2])
        z = sb("c_z", [P, 2, TB2, GW])
        ac = sb("c_ac", [P, HG, B2])
        decay = sb("c_decay", [P, HG, B2])
        chunk = sb("c_chunk", [P, HG, TB2])
        wt = sb("c_wt", [P, HG, P])
        xdt = sb("c_xdt", [P, HG, SP_])
        xend = sb("c_xend", [P, HG, SP_])
        btok = sb("c_btok", [P, NS])
        state = sb("c_state", [P, HG, SP_])
        decayed = sb("c_decayed", [P, HG, SP_])
        xd = sb("c_xd", [P, HG, SP_])
        yi = sb("c_yi", [P, HG, SP_])
        yt = sb("c_yt", [P, TB2, GW])
        yn = sb("c_yn", [P, GW])
        squares = sb("c_squares", [P, GW])
        ms = sb("c_ms", [P, TB2])
        mse = sb("c_mse", [P, TB2])
        rstd = sb("c_rstd", [P, TB2])
        neg_half = sb("c_neg_half", [P, 1])
        y = sb("c_y", [P, XT, B2])

        h_loaded = [sem(f"c_h_loaded{i}") for i in range(2)]
        h_hi = sem("c_h_hi"); h_ready = sem("c_h_ready")
        raw_loaded = [sem(f"c_raw_loaded{i}") for i in range(2)]
        passed = sem("c_passed")
        ac_loaded = sem("c_ac_loaded"); consts_ready = sem("c_consts")
        w_hi = sem("c_w_hi"); w_ready = sem("c_w_ready"); unit_done = sem("c_unit_done"); unit_out = sem("c_unit_out")
        conv_step = sem("c_conv_step"); conv_ready = sem("c_conv_ready")
        hist_ready = sem("c_hist_ready"); xbc_ready = sem("c_xbc_ready")
        seg_ready = sem("c_seg_ready"); decay_ready = sem("c_decay_ready")
        x_done = sem("c_x_done"); bc_done = sem("c_bc_done"); xdt_ready = sem("c_xdt_ready"); xend_ready = sem("c_xend_ready")
        wt_ready = sem("c_wt_ready"); y_done = sem("c_y_done"); yi_done = sem("c_yi_done"); st_done = sem("c_st_done")
        yi_ready = sem("c_yi_ready"); yt_ready = sem("c_yt_ready"); decayed_ready = sem("c_decayed_ready")
        state_ready = sem("c_state_ready"); turned = sem("c_turned"); skip_ready = sem("c_skip_ready")
        gated_ready = sem("c_gated_ready"); xd_ready = sem("c_xd_ready"); ms_ready = sem("c_ms_ready")
        mse_ready = sem("c_mse_ready"); rstd_ready = sem("c_rstd_ready"); yn_ready = sem("c_yn_ready")
        y_ready = sem("c_y_ready"); y_stored = sem("c_y_stored")

        AHEAD = 4
        H_SLOTS = (1, 2, 4, 5)

        def part(u, p):
            return w[:, u, :, p, :] if u < UZ else w_z[:, :, p, (u - UZ) * P:(u - UZ + 1) * P]

        def used(u):
            return u + 1 if u < UZ else UP

        def column(g, u):
            if u < UX:
                return CX + INNER + (u - UB) * G * NS + g * NS
            return CX + g * GW + (u - UX) * P if u < UZ else CZ + g * GW + (u - UZ) * P

        def channel(g, u):
            return INNER // P + (u - UB) * G + g if u < UX else g * XT + u - UX

        with nc.Block() as block:
            @block.sync
            def _(sp):
                def load_w(g, u):
                    wait(sp, w_ready, g * U + u - 1)
                    sp.dma_start(w_raw[:, u % 2], w_rows[:, :, column(g, u):column(g, u) + P]).then_inc(raw_loaded[u % 2], 16)

                def load_h(n, b, par, q):
                    wait(sp, h_ready, n * QS + q - 1)
                    src = h_d[bass.ds((b - par) // 2, 1)] if isinstance(b, int) else h_d[bass.ds(b // 2, 1)]
                    sp.dma_start(h_raw[:, q % 2], src[:, :, q * QK:(q + 1) * QK, par * B2:(par + 1) * B2]
                                 .rearrange("a p k n -> (a p) k n")).then_inc(h_loaded[q % 2], 16)

                def load_ac(n, g, b):
                    wait(sp, decay_ready, n)
                    sp.dma_start(ac[:, :, :], ac_d[g * HG:(g + 1) * HG, bass.ds(b * B2, B2)].partition_broadcast(P)
                                 ).then_inc(ac_loaded, 16)

                def store_y(r, g, b):
                    sp.wait_ge(y_ready, r * TB2 + TB2)
                    f = VAL // P + g * XT
                    sp.dma_start(y_d[bass.ds(b, 1), :, f:f + XT, :].rearrange("a p f n -> (a p) f n"),
                                 y[:, :, :]).then_inc(y_stored, 16)

                for u in range(U):
                    load_w(0, u)
                    if u < QS:
                        load_h(0, 0, 0, u)
                    if u == QS:
                        load_ac(0, 0, 0)
                    for q in {4: (0,), 6: (1,), 8: (2,), 9: (3,)}.get(u, ()):
                        load_h(1, 1, 1, q)

                def step(g, n, s, par, nxt):
                    if nxt is not None and not (isinstance(n, int) and n == 0):
                        for q in range(QS):
                            load_h(n + 1, nxt[1], 1 - par, q)
                            if nxt[0] != g:
                                for u in ((), (0, 1, 2, 3), (4, 5), (6, 7))[q]:
                                    load_w(g + 1, u)
                            if isinstance(s, int) and s == 0 and q == 1:
                                for u in (8, 9):
                                    load_w(g, u)
                    if nxt is not None:
                        load_ac(n + 1, *nxt)
                    if not (isinstance(s, int) and s == 0):
                        store_y(n - 1, g, s - 1)
                    elif g > 0:
                        store_y(n - 1, g - 1, S - 1)

                for g in range(G):
                    step(g, g * S, 0, 0, (g, 1))
                    step(g, g * S + 1, 1, 1, (g, 2))
                    with sp.Fori(1, S // 2 - 1) as i:
                        step(g, 2 * i + g * S, 2 * i, 0, (g, 2 * i + 1))
                        step(g, 2 * i + (g * S + 1), 2 * i + 1, 1, (g, 2 * i + 2))
                    step(g, g * S + S - 2, S - 2, 0, (g, S - 1))
                    step(g, g * S + S - 1, S - 1, 1, (g + 1, 0) if g < G - 1 else None)
                store_y(G * S - 1, G - 1, S - 1)
                sp.wait_ge(y_stored, 16 * G * S)

            @block.gpsimd
            def _(pool):
                pool.memset(past[:, :], 0.0).then_inc(consts_ready, 1)
                pool.memset(neg_half[:, :], -0.5).then_inc(consts_ready, 1)
                pool.memset(before[:, :, 0:HIST], 0.0).then_inc(consts_ready, 1)
                pool.wait_ge(consts_ready, 3)
                pool.affine_select(out=past[:, :], in_=past[:, :], compare_op=ALU.is_ge, fill=-1e30,
                                   base=0, pattern=[[1, P]], channel_multiplier=-1).then_inc(consts_ready, 1)

                def ends(r, g, b, t):
                    m = r * TB2 + t
                    pool.wait_ge(xdt_ready, m + 1)
                    wait(pool, st_done, m)
                    end = tok[:, bass.ds(b * TB2 + t, 1), 3, g * HG:(g + 1) * HG].rearrange("p a h -> p (a h)")
                    pool.tensor_tensor(xend[:, :, :], xdt[:, :, :], end.unsqueeze(2).broadcast_to([P, HG, SP_]),
                                       ALU.mult).then_inc(xend_ready, 1)

                def decay_state(r, g, t):
                    m = r * TB2 + t
                    pool.wait_ge(decay_ready, r + 1)
                    pool.wait_ge(state_ready, m + g + 1)
                    pool.tensor_tensor(decayed[:, :, :], state[:, :, :], chunk[:, :, t:t + 1].broadcast_to([P, HG, SP_]),
                                       ALU.mult).then_inc(decayed_ready, 1)

                def skip(r, t):
                    m = r * TB2 + t
                    pool.wait_ge(xd_ready, m + 1)
                    pool.wait_ge(yi_ready, m + 1)
                    pool.tensor_tensor(yi[:, :, :], yi[:, :, :], xd[:, :, :], ALU.add).then_inc(skip_ready, 1)

                def rstd_of(r, t):
                    m = r * TB2 + t
                    pool.wait_ge(ms_ready, m + 1)
                    pool.sem_inc(passed, 1)
                    pool.tensor_scalar(mse[:, t:t + 1], ms[:, t:t + 1], EPS, None, ALU.add).then_inc(mse_ready, 1)
                    pool.wait_ge(mse_ready, m + 1)
                    wait(pool, yn_ready, m)
                    pool.tensor_tensor(rstd[:, t:t + 1], mse[:, t:t + 1], neg_half[:, :], ALU.pow).then_inc(rstd_ready, 1)

                def step(r, g, b):
                    for t in range(TB2):
                        ends(r, g, b, t)
                        decay_state(r, g, t)
                        skip(r, t)
                    for t in range(TB2):
                        rstd_of(r, t)

                for g in range(G):
                    step(g * S, g, 0)
                    with pool.Fori(1, S) as i:
                        step(i + g * S, g, i)

            @block.scalar
            def _(act):

                def w_high(g, u):
                    act.wait_ge(raw_loaded[u % 2], (g * (U // 2) + u // 2 + 1) * 16)
                    wait(act, unit_done, (g * S - 1) * UP + used(u))
                    act.activation(part(u, HI), w_raw[:, u % 2], ACT.Copy).then_inc(w_hi, 1)

                def h_high(n, q, par):
                    act.wait_ge(h_loaded[q % 2], (n * (QS // 2) + q // 2 + 1) * 16)
                    wait(act, unit_done, (n - 1) * UP)
                    act.activation(hl[:, par, q * QK:(q + 1) * QK, HI, :], h_raw[:, q % 2], ACT.Copy).then_inc(h_hi, 1)

                def evacuate(n, g, u, par):
                    act.wait_ge(unit_done, n * UP + u + 1)
                    if u < UCONV:
                        wait(act, hist_ready, n)
                        ch = channel(g, u)
                        act.activation(before[:, u, HIST:], ps[:, PROJ + u % 2, 0:B2], ACT.Copy)
                        wait(act, xbc_ready, n)
                        act.activation(acc[:, u, :], ps[:, PROJ + u % 2, 0:B2], ACT.Identity,
                                       scale=conv_col[:, HIST, ch:ch + 1], bias=convb_col[:, ch:ch + 1]
                                       ).then_inc(unit_out, 1)
                    else:
                        wait(act, gated_ready, (n - 1) * TB2)
                        act.activation(z[:, par, u - UZ, :], ps[:, PROJ + u % 2, :], ACT.Silu).then_inc(unit_out, 1)

                def silu_conv(n, par):
                    act.wait_ge(conv_ready, n * UCONV + UCONV)
                    wait(act, gated_ready, (n - 1) * TB2)
                    act.activation(xbc[:, par], acc[:, :, :], ACT.Silu).then_inc(xbc_ready, 1)

                def decays(n):
                    act.wait_ge(seg_ready, n + 1)
                    wait(act, decayed_ready, n * TB2)
                    act.activation(chunk[:, :, :], ac[:, :, P - 1:B2:P], ACT.Exp)
                    act.activation(decay[:, :, :], decay[:, :, :], ACT.Exp).then_inc(decay_ready, 1)

                def square(r, t):
                    m = r * TB2 + t
                    act.wait_ge(gated_ready, m + 1)
                    wait(act, mse_ready, m)
                    wait(act, ms_ready, m)
                    act.activation(squares[:, :], yt[:, t, :], ACT.Square, scale=GW ** -0.5,
                                   accum_out=ms[:, t:t + 1]).then_inc(ms_ready, 1)

                def normed(r, t):
                    m = r * TB2 + t
                    act.wait_ge(rstd_ready, m + 1)
                    wait(act, turned, m)
                    act.activation(yn[:, :], yt[:, t, :], ACT.Copy, scale=rstd[:, t:t + 1]).then_inc(yn_ready, 1)

                def weighted(r, g, t):
                    m = r * TB2 + t
                    act.wait_ge(turned, m + 1)
                    if t == 0:
                        wait(act, y_stored, r * 16)
                    for f in range(XT):
                        k = g * XT + f
                        last = act.activation(y[:, f, t * P:(t + 1) * P], ps[:, YT, f * P:(f + 1) * P], ACT.Copy,
                                              scale=norm_col[:, k:k + 1])
                    last.then_inc(y_ready, 1)

                def step(n, g, par, rg, first, last, tail):
                    back = rg is not None
                    for u in range(UP):
                        if not tail:
                            evacuate(n, g, u, par)
                            if g == 0 and first and u + AHEAD < U:
                                w_high(0, u + AHEAD)
                            if first and g > 0 and u < XT:
                                w_high(g, UZ + u)
                            if last and g < G - 1 and u < UZ:
                                w_high(g + 1, u)
                            if u in H_SLOTS and not (last and g == G - 1):
                                h_high(n + 1, H_SLOTS.index(u), 1 - par)
                        if back and u == 3:
                            square(n - 1, 0)
                        if back and u == 4:
                            normed(n - 1, 0)
                        if back and u == 5:
                            square(n - 1, 1)
                        if u == 5 and not tail:
                            silu_conv(n, par)
                        if back and u == 6:
                            normed(n - 1, 1)
                            weighted(n - 1, rg, 0)
                        if u == 6 and not tail:
                            decays(n)
                        if back and u == 7:
                            weighted(n - 1, rg, 1)

                for u in range(AHEAD):
                    w_high(0, u)
                    h_high(0, u, 0)
                act.wait_ge(consts_ready, 4)
                for g in range(G):
                    for s in range(2):
                        step(g * S + s, g, s, g if s > 0 else g - 1 if g > 0 else None, s == 0, False, False)
                    with act.Fori(1, S // 2 - 1) as i:
                        for s in range(2):
                            step(2 * i + (g * S + s), g, s, g, False, False, False)
                    for s in range(2):
                        step(g * S + S - 2 + s, g, s, g, False, s == 1, False)
                step(G * S, G, 0, G - 1, False, True, True)

            @block.vector
            def _(dve):
                def w_low(g, u):
                    dve.wait_ge(w_hi, g * U + u + 1)
                    dve.tensor_tensor(part(u, LO), w_raw[:, u % 2], part(u, HI).bitcast(F32),
                                      ALU.subtract).then_inc(w_ready, 1)

                def h_low(n, q, par):
                    dve.wait_ge(h_hi, n * QS + q + 1)
                    ks = slice(q * QK, (q + 1) * QK)
                    dve.tensor_tensor(hl[:, par, ks, LO, :], h_raw[:, q % 2], hl[:, par, ks, HI, :].bitcast(F32),
                                      ALU.subtract).then_inc(h_ready, 1)

                def per_head(b, t, q, g):
                    cols = tok[:, bass.ds(b * TB2 + t, 1), q, g * HG:(g + 1) * HG].rearrange("p a h -> p (a h)")
                    return cols.unsqueeze(2).broadcast_to([P, HG, SP_])

                def bank(b):
                    return ps[:, b, :].rearrange("p (h w) -> p h w", w=SP_)

                def convolve(n, g, u):
                    dve.wait_ge(unit_out, n * UP + u + 1)
                    ch = channel(g, u)
                    for k in range(HIST):
                        op = dve.scalar_tensor_tensor(out=acc[:, u, :], in0=before[:, u, k:k + B2],
                                                      scalar=conv_col[:, k, ch:ch + 1], in1=acc[:, u, :],
                                                      op0=ALU.mult, op1=ALU.add)
                        if k < HIST - 1:
                            op.then_inc(conv_step, 1)
                            dve.wait_ge(conv_step, (n * UCONV + u) * (HIST - 1) + k + 1)
                    op.then_inc(conv_ready, 1)

                def history(n, s_last):
                    dve.wait_ge(conv_ready, n * UCONV + UCONV)
                    if s_last:
                        dve.memset(before[:, :, 0:HIST], 0.0).then_inc(hist_ready, 1)
                    else:
                        dve.tensor_copy(before[:, :, 0:HIST], before[:, :, B2:B2 + HIST]).then_inc(hist_ready, 1)

                def tile_in(r, g, b, t):
                    m = r * TB2 + t
                    dve.wait_ge(x_done, m + 1)
                    wait(dve, y_done, m)
                    wait(dve, xend_ready, m)
                    dve.tensor_tensor(xdt[:, :, :], bank(X), per_head(b, t, 0, g), ALU.mult).then_inc(xdt_ready, 1)
                    wait(dve, skip_ready, m)
                    skips = d_row[:, g * HG:(g + 1) * HG].unsqueeze(2).broadcast_to([P, HG, SP_])
                    dve.tensor_tensor(xd[:, :, :], bank(X), skips, ALU.mult).then_inc(xd_ready, 1)
                    dve.wait_ge(bc_done, m + 1)
                    dve.wait_ge(decay_ready, r + 1)
                    dve.tensor_tensor(wt[:, :, :], ps[:, BC, NS:NS + P].unsqueeze(1).broadcast_to([P, HG, P]),
                                      decay[:, :, t * P:(t + 1) * P], ALU.mult)
                    wait(dve, st_done, m)
                    dve.tensor_copy(btok[:, :], ps[:, BC, 0:NS]).then_inc(wt_ready, 1)

                def clear_state(r):
                    wait(dve, yi_done, r * TB2)
                    wait(dve, decayed_ready, r * TB2)
                    dve.memset(state[:, :, :], 0.0).then_inc(state_ready, 1)

                def tile_out(r, g, b, t, par):
                    m = r * TB2 + t
                    dve.wait_ge(yi_done, m + 1)
                    wait(dve, yt_ready, m)
                    dve.tensor_tensor(yi[:, :, :], bank(YI), per_head(b, t, 2, g), ALU.mult).then_inc(yi_ready, 1)
                    dve.wait_ge(st_done, m + 1)
                    dve.wait_ge(decayed_ready, m + 1)
                    dve.tensor_tensor(state[:, :, :], bank(ST), decayed[:, :, :], ALU.add).then_inc(state_ready, 1)
                    dve.wait_ge(y_done, m + 1)
                    dve.wait_ge(skip_ready, m + 1)
                    wait(dve, yn_ready, m - 1)
                    dve.tensor_tensor(yt[:, t, :].rearrange("p (h w) -> p h w", w=SP_), bank(Y), yi[:, :, :],
                                      ALU.add).then_inc(yt_ready, 1)
                    dve.wait_ge(yt_ready, m + 1)
                    dve.wait_ge(unit_out, r * UP + UP)
                    dve.tensor_tensor(yt[:, t, :], yt[:, t, :], z[:, par, t, :], ALU.mult).then_inc(gated_ready, 1)

                def segments(n, g, b):
                    dve.wait_ge(ac_loaded, n * 16 + 16)
                    wait(dve, wt_ready, n * TB2)
                    for t in range(TB2):
                        for h in range(HG):
                            k = g * HG + h
                            own = tok[:, bass.ds(b * TB2 + t, 1), 1, k:k + 1].rearrange("p a h -> p (a h)")
                            last = dve.scalar_tensor_tensor(
                                out=decay[:, h, t * P:(t + 1) * P], in0=ac[:, h, t * P:(t + 1) * P], scalar=own,
                                in1=past[:, :], op0=ALU.subtract, op1=ALU.min)
                    last.then_inc(seg_ready, 1)

                def step(n, g, b, par, rg, rb, first_of_group, last_of_group):
                    going, back = g is not None, rg is not None
                    if back and first_of_group:
                        clear_state(n - 1)
                    for u in range(UP):
                        if back and u == 0:
                            tile_in(n - 1, rg, rb, 0)
                        if back and u == 2:
                            tile_out(n - 1, rg, rb, 0, 1 - par)
                            tile_in(n - 1, rg, rb, 1)
                        if back and u == 4:
                            tile_out(n - 1, rg, rb, 1, 1 - par)
                        if going and u < UZ:
                            convolve(n, g, u)
                            if u == UZ - 1:
                                history(n, last_of_group)
                        if going and u == UZ:
                            segments(n, g, b)
                        if going and not back and u + AHEAD < U:
                            w_low(0, u + AHEAD)
                        if going and back and rg != g and u < XT:
                            w_low(g, UZ + u)
                        if last_of_group and g < G - 1 and u < UZ:
                            w_low(g + 1, u)
                        if going and u in H_SLOTS and not (last_of_group and g == G - 1):
                            h_low(n + 1, H_SLOTS.index(u), 1 - par)

                for u in range(AHEAD):
                    w_low(0, u)
                    h_low(0, u, 0)
                dve.wait_ge(consts_ready, 4)
                for g in range(G):
                    before_g = (g - 1, S - 1) if g > 0 else (None, None)
                    step(g * S, g, 0, 0, *before_g, False, False)
                    step(g * S + 1, g, 1, 1, g, 0, True, False)
                    with dve.Fori(1, S // 2 - 1) as i:
                        for s in range(2):
                            step(2 * i + (g * S + s), g, 2 * i + s, s, g, 2 * i + (s - 1), False, False)
                    step(g * S + S - 2, g, S - 2, 0, g, S - 3, False, False)
                    step(g * S + S - 1, g, S - 1, 1, g, S - 2, False, True)
                step(G * S, None, 0, 0, G - 1, S - 1, False, False)

            @block.tensor
            def _(pe):
                pe.wait_ge(consts_ready, 4)

                def unit(n, g, u, par):
                    pe.wait_ge(w_ready, g * U + (u + 1 if u < UZ else U))
                    wait(pe, unit_out, n * UP + u - 1)
                    for k in range(KT):
                        if u == 0 and k % QK == 0:
                            pe.wait_ge(h_ready, n * QS + k // QK + 1)
                        for i, (a, b) in enumerate(PASSES):
                            if u < UZ:
                                mm = pe.matmul(ps[:, PROJ + u % 2, 0:B2], w[:, u, k, a, :], hl[:, par, k, b, :],
                                               start=(k == 0 and i == 0), stop=(k == KT - 1 and i == 2))
                            else:
                                t = u - UZ
                                mm = pe.matmul(ps[:, PROJ + u % 2, :], hl[:, par, k, a, t * P:(t + 1) * P],
                                               w_z[:, k, b, :], start=(k == 0 and i == 0),
                                               stop=(k == KT - 1 and i == 2))
                    mm.then_inc(unit_done, 1)

                def tile_in(r, t, par):
                    m = r * TB2 + t
                    cols = slice(t * P, (t + 1) * P)
                    pe.wait_ge(xbc_ready, r + 1)
                    wait(pe, xd_ready, m)
                    for f in range(XT):
                        mm = pe.transpose(ps[:, X, f * P:(f + 1) * P], xbc[:, par, UX + f, cols], ident[:, :])
                    mm.then_inc(x_done, 1)
                    wait(pe, wt_ready, m)
                    pe.transpose(ps[:, BC, 0:NS], xbc[:, par, UB, cols], ident[:, :])
                    pe.matmul(ps[:, BC, NS:NS + P], xbc[:, par, UB, cols], xbc[:, par, UC, cols], start=True,
                              stop=True).then_inc(bc_done, 1)

                def tile_out(r, g, t, par):
                    m = r * TB2 + t
                    pe.wait_ge(state_ready, m + g + 1)
                    wait(pe, yi_ready, m)
                    pe.matmul(ps[:, YI, :], xbc[:, par, UC, t * P:(t + 1) * P],
                              state[:, :, :].rearrange("p h w -> p (h w)"), start=True, stop=True).then_inc(yi_done, 1)
                    pe.wait_ge(wt_ready, m + 1)
                    pe.wait_ge(xdt_ready, m + 1)
                    wait(pe, yt_ready, m)
                    for h in range(HG):
                        mm = pe.matmul(ps[:, Y, h * SP_:(h + 1) * SP_], wt[:, h, :], xdt[:, h, :], start=True, stop=True)
                    mm.then_inc(y_done, 1)
                    pe.wait_ge(xend_ready, m + 1)
                    pe.matmul(ps[:, ST, :], btok[:, :], xend[:, :, :].rearrange("p h w -> p (h w)"), start=True,
                              stop=True).then_inc(st_done, 1)

                def turn(r, t):
                    m = r * TB2 + t
                    pe.wait_ge(yn_ready, m + 1)
                    wait(pe, y_ready, m)
                    for f in range(XT):
                        mm = pe.transpose(ps[:, YT, f * P:(f + 1) * P], yn[:, f * P:(f + 1) * P], ident[:, :])
                    mm.then_inc(turned, 1)

                def step(n, g, par, rg):
                    going, back = g is not None, rg is not None
                    for u in range(UP):
                        if back and u == 0:
                            tile_in(n - 1, 0, 1 - par)
                        if back and u == 2:
                            tile_out(n - 1, rg, 0, 1 - par)
                            tile_in(n - 1, 1, 1 - par)
                        if back and u == 4:
                            tile_out(n - 1, rg, 1, 1 - par)
                        if back and u == 6:
                            turn(n - 1, 0)
                        if going:
                            unit(n, g, u, par)
                    if back:
                        turn(n - 1, 1)

                for g in range(G):
                    step(g * S, g, 0, g - 1 if g > 0 else None)
                    step(g * S + 1, g, 1, g)
                    with pe.Fori(1, S // 2) as i:
                        for s in range(2):
                            step(2 * i + (g * S + s), g, s, g)
                step(G * S, None, 0, G - 1)


def project_out(nc, x, w_out, out, ps, gate_d, y_d, D, FT, NB2, B2, TB2):
    HALVES = D // 512
    FQ = FT // 4
    FIRST_SLOTS = (0, FQ - 2, 2 * FQ - 2, 3 * FQ - 2)
    with ExitStack() as ctx:
        def sb(name, shape, dt=F32):
            return ctx.enter_context(nc.sbuf_tensor(name, shape, dt))

        def sem(name):
            return ctx.enter_context(nc.semaphore(name))

        w = sb("d_w", [P, FT, 2, D], F32R)
        w_raw = sb("d_w_raw", [P, 2, D])
        gate_row = sb("d_gate_row", [P, D])
        y_raw = sb("d_y_raw", [P, FT, B2])
        yh = sb("d_yh", [P, TB2, FT, 2, P], F32R)
        x_sb = sb("d_x", [P, TB2, D])
        squares = sb("d_squares", [P, D])
        scaled = sb("d_scaled", [P, D])
        ms = sb("d_ms", [P, 1])
        mse = sb("d_mse", [P, 1])
        rstd = sb("d_rstd", [P, 1])
        neg_half = sb("d_neg_half", [P, 1])
        raw_loaded = [sem(f"d_raw_loaded{i}") for i in range(2)]
        x_loaded = [sem(f"d_x_loaded{i}") for i in range(TB2)]
        passed = sem("d_passed")
        w_hi = sem("d_w_hi"); w_ready = sem("d_w_ready"); consts_ready = sem("d_consts"); gate_loaded = sem("d_gate_loaded")
        y_loaded = sem("d_y_loaded"); first_loaded = [sem(f"d_first_loaded{i}") for i in range(2)]
        first_hi = sem("d_first_hi"); first_ready = sem("d_first_ready"); y_hi = sem("d_y_hi"); y_ready = sem("d_y_ready"); mixed_done = sem("d_mixed_done")
        ms_ready = sem("d_ms_ready"); mse_ready = sem("d_mse_ready"); rstd_ready = sem("d_rstd_ready")
        scaled_ready = sem("d_scaled_ready"); sum_ready = sem("d_sum_ready"); stored = [sem(f"d_stored{i}") for i in range(TB2)]

        with nc.Block() as block:
            @block.sync
            def _(sp):
                def load_x(b, t):
                    wait(sp, stored[t], b * 16)
                    rows = x[0, bass.ds(b * B2 + t * P, P), :]
                    sp.dma_start(x_sb[:, t, :], rows).then_inc(x_loaded[t], 16)

                def load_first_y(i):
                    sp.dma_start(y_raw[:, i * FQ:(i + 1) * FQ, :], y_d[0, :, i * FQ:(i + 1) * FQ, :]).then_inc(first_loaded[i % 2], 16)

                def load_y(b):
                    if isinstance(b, int):
                        sp.wait_ge(first_ready, FT // FQ * TB2)
                    else:
                        sp.wait_ge(y_ready, (b - 1) * TB2)
                    sp.dma_start(y_raw[:, :, :], y_d[bass.ds(b, 1)].rearrange("a p f n -> (a p) f n")).then_inc(y_loaded, 16)

                def load_w(f):
                    wait(sp, w_ready, f - 1)
                    sp.dma_start(w_raw[:, f % 2, :], w_out[0, f * P:(f + 1) * P, :]).then_inc(raw_loaded[f % 2], 16)

                for f in range(FT):
                    load_w(f)
                    if f in FIRST_SLOTS:
                        load_first_y(FIRST_SLOTS.index(f))
                load_y(1)
                sp.dma_start(gate_row[:, :], gate_d[0].partition_broadcast(P)).then_inc(gate_loaded, 16)
                for t in range(TB2):
                    load_x(0, t)

                def store(b, t):
                    sp.wait_ge(sum_ready, b * TB2 + t + 1)
                    sp.dma_start(out[0, bass.ds(b * B2 + t * P, P), :], x_sb[:, t, :]).then_inc(stored[t], 16)

                for t in range(TB2):
                    store(0, t)
                    load_x(1, t)
                with sp.Fori(1, NB2 - 1) as b:
                    load_y(b + 1)
                    for t in range(TB2):
                        store(b, t)
                        load_x(b + 1, t)
                for t in range(TB2):
                    store(NB2 - 1, t)
                for t in range(TB2):
                    sp.wait_ge(stored[t], 16 * NB2)

            @block.gpsimd
            def _(pool):
                pool.memset(neg_half[:, :], -0.5).then_inc(consts_ready, 1)
                pool.wait_ge(consts_ready, 1)

                def rstd_of(m):
                    pool.wait_ge(ms_ready, m + 1)
                    wait(pool, rstd_ready, m)
                    pool.sem_inc(passed, 1)
                    pool.tensor_scalar(mse[:, :], ms[:, :], EPS, None, ALU.add).then_inc(mse_ready, 1)
                    pool.wait_ge(mse_ready, m + 1)
                    wait(pool, scaled_ready, m)
                    pool.tensor_tensor(rstd[:, :], mse[:, :], neg_half[:, :], ALU.pow).then_inc(rstd_ready, 1)

                rstd_of(0)
                with pool.Fori(1, NB2 * TB2) as m:
                    rstd_of(m)

            @block.scalar
            def _(act):
                def split_first(i, t):
                    if t == 0:
                        act.wait_ge(first_loaded[i % 2], (i // 2 + 1) * 16)
                    fs = slice(i * FQ, (i + 1) * FQ)
                    act.activation(yh[:, t, fs, HI, :], y_raw[:, fs, t * P:(t + 1) * P], ACT.Copy).then_inc(first_hi, 1)

                def split_y(b, t):
                    if t == 0:
                        act.wait_ge(y_loaded, b * 16)
                    wait(act, mixed_done, b * TB2 + t - (TB2 - 1))
                    act.activation(yh[:, t, :, HI, :], y_raw[:, :, t * P:(t + 1) * P], ACT.Copy).then_inc(y_hi, 1)

                def square(m, t):
                    act.wait_ge(mixed_done, m + 1)
                    wait(act, mse_ready, m)
                    wait(act, ms_ready, m)
                    act.activation(squares[:, :], ps[:, 2 * t:2 * t + 2, :].rearrange("p a n -> p (a n)"), ACT.Square,
                                   scale=D ** -0.5, accum_out=ms[:, :]).then_inc(ms_ready, 1)

                for f in range(FT):
                    act.wait_ge(raw_loaded[f % 2], (f // 2 + 1) * 16)
                    act.activation(w[:, f, HI, :], w_raw[:, f % 2, :], ACT.Copy).then_inc(w_hi, 1)
                    if f in FIRST_SLOTS:
                        for t in range(TB2):
                            split_first(FIRST_SLOTS.index(f), t)
                for t in range(TB2):
                    split_y(1, t)
                    square(t, t)
                with act.Fori(1, NB2 - 1) as b:
                    for t in range(TB2):
                        square(b * TB2 + t, t)
                        split_y(b + 1, t)
                for t in range(TB2):
                    square((NB2 - 1) * TB2 + t, t)

            @block.vector
            def _(dve):
                def split_first(i, t):
                    dve.wait_ge(first_hi, i * TB2 + t + 1)
                    fs = slice(i * FQ, (i + 1) * FQ)
                    dve.tensor_tensor(yh[:, t, fs, LO, :], y_raw[:, fs, t * P:(t + 1) * P],
                                      yh[:, t, fs, HI, :].bitcast(F32), ALU.subtract).then_inc(first_ready, 1)

                def split_y(b, t):
                    dve.wait_ge(y_hi, (b - 1) * TB2 + t + 1)
                    dve.tensor_tensor(yh[:, t, :, LO, :], y_raw[:, :, t * P:(t + 1) * P],
                                      yh[:, t, :, HI, :].bitcast(F32), ALU.subtract).then_inc(y_ready, 1)

                def finish(b, t):
                    m = b * TB2 + t
                    dve.wait_ge(rstd_ready, m + 1)
                    wait(dve, sum_ready, m)
                    dve.scalar_tensor_tensor(out=scaled[:, :], in0=ps[:, 2 * t:2 * t + 2, :].rearrange("p a n -> p (a n)"),
                                             scalar=rstd[:, :], in1=gate_row[:, :], op0=ALU.mult,
                                             op1=ALU.mult).then_inc(scaled_ready, 1)
                    dve.wait_ge(scaled_ready, m + 1)
                    dve.wait_ge(x_loaded[t], b * 16 + 16)
                    dve.tensor_tensor(x_sb[:, t, :], x_sb[:, t, :], scaled[:, :], ALU.add).then_inc(sum_ready, 1)

                for f in range(FT):
                    dve.wait_ge(w_hi, f + 1)
                    dve.tensor_tensor(w[:, f, LO, :], w_raw[:, f % 2, :], w[:, f, HI, :].bitcast(F32),
                                      ALU.subtract).then_inc(w_ready, 1)
                    if f in FIRST_SLOTS:
                        for t in range(TB2):
                            split_first(FIRST_SLOTS.index(f), t)
                dve.wait_ge(gate_loaded, 16)
                for t in range(TB2):
                    split_y(1, t)
                    finish(0, t)
                with dve.Fori(1, NB2 - 1) as b:
                    for t in range(TB2):
                        finish(b, t)
                        split_y(b + 1, t)
                for t in range(TB2):
                    finish(NB2 - 1, t)

            @block.tensor
            def _(pe):
                def products(t, f):
                    for i, (a, c) in enumerate(PASSES):
                        for j in range(HALVES):
                            mm = pe.matmul(ps[:, 2 * t + j, :], yh[:, t, f, a, :], w[:, f, c, j * 512:(j + 1) * 512],
                                           start=(f == 0 and i == 0), stop=(f == FT - 1 and i == 2))
                    if f == FT - 1:
                        mm.then_inc(mixed_done, 1)

                for i in range(FT // FQ):
                    for t in range(TB2):
                        pe.wait_ge(first_ready, i * TB2 + t + 1)
                        for f in range(i * FQ, (i + 1) * FQ):
                            if t == 0:
                                pe.wait_ge(w_ready, f + 1)
                            products(t, f)
                with pe.Fori(1, NB2) as b:
                    for t in range(TB2):
                        m = b * TB2 + t
                        pe.wait_ge(y_ready, m - TB2 + 1)
                        pe.wait_ge(scaled_ready, m - (TB2 - 1))
                        for f in range(FT):
                            products(t, f)


_INS = ["x", "c", "ada_w", "ada_b", "pre_norm_w", "w_in", "gla_gate_w2", "gla_gate_b", "gla_norm_w", "conv_w", "conv_b",
        "dt_bias", "a_log", "d_skip", "ssd_norm_w", "w_out", "post_norm_w"]


def kernel(**inputs):
    import numpy as np
    import concourse.bacc as bacc
    from concourse.bass_utils import run_bass_kernel_spmd

    nc = bacc.Bacc("TRN2", target_bir_lowering=False, num_devices=1)
    arrays, args = {}, []
    for name in _INS:
        a = np.ascontiguousarray(inputs[name])
        arrays[f"in_{name}"] = a
        args.append(nc.dram_tensor(f"in_{name}", a.shape, mybir.dt.from_np(a.dtype), kind="ExternalInput").ap())
    shape = inputs["x"].shape
    args.append(nc.dram_tensor("out", shape, F32, kind="ExternalOutput").ap())
    build(nc, *args)
    return run_bass_kernel_spmd(nc, [arrays], core_ids=[0]).results[0]["out"]
```
